# Optimizing a Trainium2 kernel written in Bass

```python
import math
import jax
import jax.numpy as jnp
from jax import lax
import numpy as np

D_MODEL = 2048
BATCH = 1
SEQ = 256
DEPTH = 1

POOL_WIDTH = D_MODEL // 2
POOL_WINDOWS = (2, 4, 8, 16)
POOL_GROUPS = len(POOL_WINDOWS)
POOL_GROUP_DIM = POOL_WIDTH // POOL_GROUPS
DIFF_HEADS = 8
DIFF_HEAD_DIM = D_MODEL // (4 * DIFF_HEADS)
DIFF_V_DIM = 2 * DIFF_HEAD_DIM
ATTN_WIDTH = DIFF_HEADS * DIFF_V_DIM
IN_WIDTH = POOL_WIDTH + 3 * ATTN_WIDTH
Q_BLOCK = 128
REL_BUCKETS = 32
REL_MAX_DISTANCE = 128
N_GROUPS = 4
EXPERTS_PER_GROUP = 8
N_EXPERTS = N_GROUPS * EXPERTS_PER_GROUP
TOP_K_IN_GROUP = 2
D_EXPERT = D_MODEL // 4
EPS = 1e-6
NEG_INF = -1e30

kernel_name = "hybrid_pool_diffattn_hmoe"

def rms_norm(x, gain, eps=EPS):
    xf = x.astype(jnp.float32)
    y = xf * lax.rsqrt(jnp.mean(xf * xf, axis=-1, keepdims=True) + eps)
    return (y * gain.astype(jnp.float32)).astype(x.dtype)

def relative_bucket(q_pos, k_pos):
    n = jnp.maximum(q_pos[:, None] - k_pos[None, :], 0)
    max_exact = REL_BUCKETS // 2
    nf = jnp.maximum(n, 1).astype(jnp.float32)
    large = max_exact + (jnp.log(nf / max_exact) / math.log(REL_MAX_DISTANCE / max_exact)
                         * (REL_BUCKETS - max_exact)).astype(jnp.int32)
    large = jnp.minimum(large, REL_BUCKETS - 1)
    return jnp.where(n < max_exact, n, large)

def pool_mixer(u, w_mix, scale):
    B, S, _ = u.shape
    ug = u.reshape(B, S, POOL_GROUPS, POOL_GROUP_DIM).astype(jnp.float32)
    csum = jnp.cumsum(ug, axis=1)
    t = jnp.arange(S)
    outs = []
    for g, w in enumerate(POOL_WINDOWS):
        c = csum[:, :, g]
        lagged = jnp.pad(c, ((0, 0), (w, 0), (0, 0)))[:, :S]
        count = jnp.minimum(t + 1, w).astype(jnp.float32)[None, :, None]
        outs.append((c - lagged) / count - ug[:, :, g])
    pooled = jnp.stack(outs, axis=2).astype(u.dtype)
    mixed = jnp.einsum('bsgc,gcd->bsgd', pooled, w_mix).reshape(B, S, POOL_WIDTH)
    return mixed * scale

def diff_attention(q, k, v, rel_table, lam, subln_gain, lambda_init):
    B, S = q.shape[:2]
    q = q * (DIFF_HEAD_DIM ** -0.5)
    pos = jnp.arange(S)
    outs = []
    for start in range(0, S, Q_BLOCK):
        end = start + Q_BLOCK
        qb = q[:, start:end]
        kb = k[:, :end]
        vb = v[:, :end]
        logits = jnp.einsum('bqhcd,bkhcd->bhcqk', qb, kb,
                            preferred_element_type=jnp.float32)
        q_pos = pos[start:end]
        k_pos = pos[:end]
        bias = rel_table[relative_bucket(q_pos, k_pos)].astype(jnp.float32)
        bias = jnp.transpose(bias, (2, 0, 1))[None, :, None]
        causal = k_pos[None, :] <= q_pos[:, None]
        logits = jnp.where(causal, logits + bias, NEG_INF)
        p = jax.nn.softmax(logits, axis=-1)
        a = (p[:, :, 0] - lam * p[:, :, 1]).astype(v.dtype)
        outs.append(jnp.einsum('bhqk,bkhe->bqhe', a, vb))
    o = jnp.concatenate(outs, axis=1)
    o = rms_norm(o, subln_gain) * (1.0 - lambda_init)
    return o.reshape(B, S, ATTN_WIDTH)

def mixer_block(xn, layer_idx, rel_table, w_in, w_merge_gate, b_merge_gate, pool_mix, pool_scale,
                w_up_pool, lambda_q1, lambda_k1, lambda_q2, lambda_k2, subln_gain, w_up_attn, w_out):
    B, S, _ = xn.shape
    proj = xn @ w_in
    u_pool, q, k, v = jnp.split(
        proj, [POOL_WIDTH, POOL_WIDTH + ATTN_WIDTH, POOL_WIDTH + 2 * ATTN_WIDTH], axis=-1)
    q = q.reshape(B, S, DIFF_HEADS, 2, DIFF_HEAD_DIM)
    k = k.reshape(B, S, DIFF_HEADS, 2, DIFF_HEAD_DIM)
    v = v.reshape(B, S, DIFF_HEADS, DIFF_V_DIM)
    y_pool = pool_mixer(u_pool, pool_mix, pool_scale) @ w_up_pool
    lambda_init = 0.8 - 0.6 * math.exp(-0.3 * layer_idx)
    lam = (jnp.exp(jnp.sum(lambda_q1.astype(jnp.float32) * lambda_k1.astype(jnp.float32)))
           - jnp.exp(jnp.sum(lambda_q2.astype(jnp.float32) * lambda_k2.astype(jnp.float32)))
           + lambda_init)
    y_attn = diff_attention(q, k, v, rel_table, lam, subln_gain, lambda_init) @ w_up_attn
    gates = jax.nn.sigmoid(xn @ w_merge_gate + b_merge_gate)
    g_pool, g_attn = jnp.split(gates, 2, axis=-1)
    return (g_pool * y_pool + g_attn * y_attn) @ w_out

def hierarchical_moe(x, w_rg, b_rg, w_re, b_re, w_gate, w_up, w_down):
    B, S, D = x.shape
    N = B * S
    xt = x.reshape(N, D)
    g_logits = (xt @ w_rg + b_rg).astype(jnp.float32)
    g_prob = jax.nn.softmax(g_logits, axis=-1)
    g_sel = jnp.argmax(g_logits, axis=-1)
    g_weight = jnp.take_along_axis(g_prob, g_sel[:, None], axis=-1)
    e_logits_all = (jnp.einsum('nd,gde->nge', xt, w_re) + b_re).astype(jnp.float32)
    e_logits = jnp.take_along_axis(e_logits_all, g_sel[:, None, None], axis=1)[:, 0]
    top_vals, top_idx = lax.top_k(e_logits, TOP_K_IN_GROUP)
    top_w = jax.nn.softmax(top_vals, axis=-1) * g_weight
    expert_id = g_sel[:, None] * EXPERTS_PER_GROUP + top_idx
    combine = jnp.sum(jax.nn.one_hot(expert_id, N_EXPERTS, dtype=jnp.float32)
                      * top_w[..., None], axis=1).astype(x.dtype)
    y = jnp.zeros((N, D), x.dtype)
    for g in range(N_GROUPS):
        sl = slice(g * EXPERTS_PER_GROUP, (g + 1) * EXPERTS_PER_GROUP)
        h = (jax.nn.silu(jnp.einsum('nd,edf->nef', xt, w_gate[sl]))
             * jnp.einsum('nd,edf->nef', xt, w_up[sl]))
        h = h * combine[:, sl, None]
        y = y + jnp.einsum('nef,efd->nd', h, w_down[sl])
    return y.reshape(B, S, D)

def setup_inputs(seed: int = 0) -> dict:
    key = jax.random.key(seed)
    ks = jax.random.split(key, 32)
    f32 = jnp.float32

    def nrm(k, shape, fan_in):
        return jax.random.normal(k, shape, f32) * fan_in ** -0.5

    def gain(k, shape):
        return 1.0 + 0.02 * jax.random.normal(k, shape, f32)

    def small(k, shape, s):
        return s * jax.random.normal(k, shape, f32)

    return {
        "x": jax.random.normal(ks[0], (BATCH, SEQ, D_MODEL), f32),
        "rel_bias_table": small(ks[1], (REL_BUCKETS, DIFF_HEADS), 0.5),
        "norm_mix_gain": gain(ks[2], (DEPTH, D_MODEL)),
        "w_in": nrm(ks[3], (DEPTH, D_MODEL, IN_WIDTH), D_MODEL),
        "w_merge_gate": nrm(ks[4], (DEPTH, D_MODEL, 2 * D_MODEL), D_MODEL),
        "b_merge_gate": small(ks[5], (DEPTH, 2 * D_MODEL), 0.02),
        "pool_mix": nrm(ks[6], (DEPTH, POOL_GROUPS, POOL_GROUP_DIM, POOL_GROUP_DIM), POOL_GROUP_DIM),
        "pool_scale": gain(ks[7], (DEPTH, POOL_WIDTH)),
        "w_up_pool": nrm(ks[8], (DEPTH, POOL_WIDTH, D_MODEL), POOL_WIDTH),
        "lambda_q1": small(ks[9], (DEPTH, DIFF_HEAD_DIM), 0.1),
        "lambda_k1": small(ks[10], (DEPTH, DIFF_HEAD_DIM), 0.1),
        "lambda_q2": small(ks[11], (DEPTH, DIFF_HEAD_DIM), 0.1),
        "lambda_k2": small(ks[12], (DEPTH, DIFF_HEAD_DIM), 0.1),
        "subln_gain": gain(ks[13], (DEPTH, DIFF_V_DIM)),
        "w_up_attn": nrm(ks[14], (DEPTH, ATTN_WIDTH, D_MODEL), ATTN_WIDTH),
        "w_out": nrm(ks[15], (DEPTH, D_MODEL, D_MODEL), D_MODEL),
        "norm_ffn_gain": gain(ks[16], (DEPTH, D_MODEL)),
        "w_router_group": nrm(ks[17], (DEPTH, D_MODEL, N_GROUPS), D_MODEL),
        "b_router_group": small(ks[18], (DEPTH, N_GROUPS), 0.01),
        "w_router_expert": nrm(ks[19], (DEPTH, N_GROUPS, D_MODEL, EXPERTS_PER_GROUP), D_MODEL),
        "b_router_expert": small(ks[20], (DEPTH, N_GROUPS, EXPERTS_PER_GROUP), 0.01),
        "w_expert_gate": nrm(ks[21], (DEPTH, N_EXPERTS, D_MODEL, D_EXPERT), D_MODEL),
        "w_expert_up": nrm(ks[22], (DEPTH, N_EXPERTS, D_MODEL, D_EXPERT), D_MODEL),
        "w_expert_down": nrm(ks[23], (DEPTH, N_EXPERTS, D_EXPERT, D_MODEL), D_EXPERT),
        "final_norm_gain": gain(ks[24], (D_MODEL,)),
    }

def reference(x, rel_bias_table, norm_mix_gain, w_in, w_merge_gate, b_merge_gate, pool_mix,
              pool_scale, w_up_pool, lambda_q1, lambda_k1, lambda_q2, lambda_k2, subln_gain,
              w_up_attn, w_out, norm_ffn_gain, w_router_group, b_router_group, w_router_expert,
              b_router_expert, w_expert_gate, w_expert_up, w_expert_down, final_norm_gain):
    h = x
    for l in range(DEPTH):
        xn = rms_norm(h, norm_mix_gain[l])
        h = h + mixer_block(xn, l, rel_bias_table, w_in[l], w_merge_gate[l], b_merge_gate[l],
                            pool_mix[l], pool_scale[l], w_up_pool[l], lambda_q1[l], lambda_k1[l],
                            lambda_q2[l], lambda_k2[l], subln_gain[l], w_up_attn[l], w_out[l])
        hn = rms_norm(h, norm_ffn_gain[l])
        h = h + hierarchical_moe(hn, w_router_group[l], b_router_group[l], w_router_expert[l],
                                 b_router_expert[l], w_expert_gate[l], w_expert_up[l],
                                 w_expert_down[l])
    return rms_norm(h, final_norm_gain)


_drawn_inputs = setup_inputs


def setup_inputs(seed=0):
    import zlib

    import numpy as np

    out = dict(_drawn_inputs(seed))
    spreads = {}
    factors = {'b_merge_gate': 4.343,
     'pool_scale': 9.204,
     'lambda_q1': 3.133,
     'lambda_k1': 8.0,
     'subln_gain': 10.138,
     'b_router_group': 14.668,
     'b_router_expert': 14.665,
     'final_norm_gain': 8.028,
     'lambda_q2': 3.142,
     'lambda_k2': 5.431,
     'norm_ffn_gain': 3.631}
    for name, (base, spread) in spreads.items():
        noise = np.random.default_rng([zlib.crc32(name.encode()), seed]).standard_normal(out[name].shape)
        drawn = base * np.exp(spread * noise) if base else spread * noise
        out[name] = jnp.asarray(drawn.astype(out[name].dtype))
    for name, factor in factors.items():
        out[name] = (out[name] * factor).astype(out[name].dtype)
    return out
```

```python
from contextlib import ExitStack

import concourse.bass as bass
from concourse import mybir

F32 = mybir.dt.float32
F32R = mybir.dt.float32r
I32 = mybir.dt.int32
U32 = mybir.dt.uint32
ALU = mybir.AluOpType
ACT = mybir.ActivationFunctionType
AX = mybir.AxisListType.X

P = 128
TOK = 256
TT = TOK // P
D = 2048
KT = D // P
BLK = 1024
BANK = 512
RING = 4
UNIT = 4096
POOL_W = 1024
WINDOWS = (2, 4, 8, 16)
HEADS = 8
DH = 64
NEG = -1e30
EPS = 1e-6
LAMBDA_INIT = 0.2
N_GROUPS = 4
N_EXP = 32
F_EXP = 512
CAP = 64
PAIRS = N_EXP // 2
PASSES = TOK // CAP
PAIR_UNITS = 12
MIX_UNITS = 48
NG = 3
NQ = 4
FILLS = KT // 2
BIG = 1000.0


class Chain:

    def __init__(self, eng, sem):
        self.eng, self.sem, self.base, self.k, self.outer = eng, sem, 0, 0, []

    def step(self, ins):
        ins.then_inc(self.sem, 1)
        self.k += 1

    def settle(self):
        self.eng.wait_ge(self.sem, self.base + self.k)

    def enter(self, i, steps):
        self.outer.append((self.base, self.k, steps))
        self.base, self.k = self.base + self.k + i * steps, 0

    def leave(self, count):
        base, k, steps = self.outer.pop()
        assert self.k == steps, (self.k, steps)
        self.base, self.k = base, k + count * steps


def pair_units():
    return ([(k, e, h) for e in range(2) for k in ("gate", "up") for h in range(2)]
            + [("down", e, h) for e in range(2) for h in range(2)])


def build(nc, t):
    with ExitStack() as ctx:
        def sem(name):
            return ctx.enter_context(nc.semaphore(name))

        ctx.enter_context(nc.sbuf_tensor("fence", [P, 207 * 256], F32))
        first = 16512

        def at(name, kib, shape, dtype=F32):
            size = 4
            for n in shape[1:]:
                size *= n
            assert kib * 1024 + size <= 207 * 1024
            return nc.alloc_sbuf_tensor_at(name, shape, dtype, offset=first + int(kib * 1024))

        ring = at("ring", 0, [P, RING, UNIT])
        xT = at("xT", 64, [P, KT, TOK])
        x_in = at("x_in", 80, [P, TT, D])
        hankel = at("hankel", 96, [P, HEADS, 256])
        bias_rows = at("bias_rows", 104, [HEADS, BANK])
        onehot = at("onehot", 106, [33, BANK])
        table = at("table", 108, [33, HEADS])
        lam_in = at("lam_in", 109, [P, 4, DH])
        lam_prod = at("lam_prod", 110, [P, 2, DH])
        flip = at("flip", 111, [P, P])
        proj = at("proj", 80, [P, TT, 4 * BLK])
        pool_at = at("pool_at", 112, [P, TT, 4, TOK])
        w_mix = at("w_mix", 120, [P, 8, 256])
        pooledT = at("pooledT", 128, [P, 8, TOK])
        gates = at("gates", 112, [P, TT, 4 * BLK])
        b_gate = at("b_gate", 144, [P, 4 * BLK])
        bias = at("bias", 160, [P, HEADS, 384])
        mixedT = at("mixedT", 172, [P, 8, TOK])
        oT = at("oT", 180, [P, HEADS, TOK])
        qk = at("qk", 188, [P, 2, TT, P])
        qkT = at("qkT", 190, [P, 2, TOK])
        probs = at("probs", 192, [P, 2, 384])
        amap = at("amap", 195, [P, 384])
        amapT = at("amapT", 196.5, [P, 384])
        o_n = at("o_n", 198, [P, TT, P])
        o_sq = at("o_sq", 199, [P, TT, P])
        merged = at("merged", 80, [P, TT, D])
        x_again = at("x_again", 96, [P, TT, D])
        mergedT = at("mergedT", 64, [P, KT, TOK])
        h = at("h", 144, [P, TT, D])
        ident = at("ident", 200, [P, P])
        iota = at("iota", 200.5, [P, P])
        w_rout = at("w_rout", 201, [P, KT, 36])
        small = at("small", 203.5, [P, 192])
        tri = at("tri", 204.5, [P, P])
        ones = at("ones", 205, [P, P])
        gain_ffn = at("gain_ffn", 188, [P, D])
        hn = at("hn", 80, [P, TT, D])
        hnT = at("hnT", 64, [P, KT, TOK])
        rt = at("rt", 160, [P, TT, 8, 36])
        hn_hi = at("hn_hi", 112, [P, TT, KT, P], F32R)
        hn_lo = at("hn_lo", 128, [P, TT, KT, P], F32R)
        xg = at("xg", 64, [P, 2 * KT, 2, CAP], F32R)
        w_hi = at("w_hi", 80, [P, NQ, 1024], F32R)
        w_lo = at("w_lo", 96, [P, NQ, 1024], F32R)
        sel = at("sel", 163, [P, TT, P], F32R)
        sel_a = at("sel_a", 164, [P, TT, P])
        part = at("part", 165, [CAP, BANK])
        g_sb = at("g_sb", 167, [CAP, BANK])
        u_sb = at("u_sb", 169, [CAP, BANK])
        silu_g = at("silu_g", 171, [CAP, BANK])
        hid = at("hid", 173, [CAP, BANK])
        y_part = at("y_part", 175, [CAP, 2 * BANK])
        hidT = at("hidT", 179, [P, 2, 4, P], F32R)
        y_sb = at("y_sb", 188, [P, D])
        rows = at("rows", 196, [P, TT, 2], U32)
        count = at("count", 196.25, [P, 1], I32)
        code = at("code", 196.5, [P, TT, 2])
        topw = at("topw", 197, [P, TT, 2])
        topw_now = at("topw_now", 197.25, [P, TT, 2])
        in_pass = at("in_pass", 197.5, [P, TT, 2])
        fetched = at("fetched", 64, [P, TT, 2, D])
        gain_out = at("gain_out", 96, [P, D])

        gain_mix = small[:, 0:16]
        pool_scale = small[:, 16:24]
        subln = small[:, 24:25]
        stat = small[:, 32:64]
        b_rout = small[:, 64:100]
        lam_s = small[:, 100:108]
        sums = small[:, 108:112]
        nmax = small[:, 112:116]
        inv = small[:, 116:120]
        coef = small[:, 120:122]
        ssq_o = small[:, 122:124]
        var_o = small[:, 124:126]
        std_o = small[:, 126:128]
        inv_o = small[:, 128:130]
        nlam = small[:, 130:131]
        gain_o = small[:, 131:132]

        bank = ctx.enter_context(nc.psum_tensor("bank", [P, 8, BANK], F32))

        landed = [sem(f"landed{i}") for i in range(RING)]
        unit_free = sem("unit_free")
        x_ld, id_ld, tab_ld, sm_ld, lam_ld = (sem(n) for n in ("x_ld", "id_ld", "tab_ld", "sm_ld", "lam_ld"))
        pool_ld, bg_ld, hankel_ld, bias_st = (sem(n) for n in ("pool_ld", "bg_ld", "hankel_ld", "bias_st"))
        x2_ld, gffn_ld, rout_ld, gout_ld = (sem(n) for n in ("x2_ld", "gffn_ld", "rout_ld", "gout_ld"))
        dve_c, last_c = sem("dve_chain"), sem("dve_last")
        table_ok, bias_row_ps, bias_row_sb, flip_ps, bias_ok = (
            sem(n) for n in ("table_ok", "bias_row_ps", "bias_row_sb", "flip_ps", "bias_ok"))
        ssq1, var1, std1, inv1, xs_ok, xT_ps = (sem(n) for n in ("ssq1", "var1", "std1", "inv1", "xs_ok", "xT_ps"))
        emptied_a, emptied_d = sem("emptied_a"), sem("emptied_d")
        pooled_ps, low_free, mixed_ps, bank7_free = (
            sem(n) for n in ("pooled_ps", "low_free", "mixed_ps", "bank7_free"))
        lam_dot, lam_exp = sem("lam_dot"), sem("lam_exp")
        staged, qkT_ps, qkT_ok, s_ps, s_free, nmax_ok, p_ok = (
            sem(n) for n in ("staged", "qkT_ps", "qkT_ok", "s_ps", "s_free", "nmax_ok", "p_ok"))
        a_ok, aT_ps, aT_ok, o_ps, ssq_ok, var_ok, std_ok, on_ok, oT_ps = (
            sem(n) for n in ("a_ok", "aT_ps", "aT_ok", "o_ps", "ssq_ok", "var_ok", "std_ok", "on_ok", "oT_ps"))
        sig_ok, up_free, merged_ok, mT_ps, mT_a, mT_d, h_ok = (
            sem(n) for n in ("sig_ok", "up_free", "merged_ok", "mT_ps", "mT_a", "mT_d", "h_ok"))
        ssq2, var2, std2, inv2, hs_ok, hn_ok, hnT_ps, hnT_a, hnT_d, hi_ok, lo_ok = (
            sem(n) for n in ("ssq2", "var2", "std2", "inv2", "hs_ok", "hn_ok", "hnT_ps", "hnT_a", "hnT_d",
                             "hi_ok", "lo_ok"))
        logit_ps, gdiff, gexp, mdiff, mexp, mask_ok, rank_ps, route_ok = (
            sem(n) for n in ("logit_ps", "gdiff", "gexp", "mdiff", "mexp", "mask_ok", "rank_ps", "route_ok"))
        sel_ok, gath_ps, gath_a, gath_d = (sem(n) for n in ("sel_ok", "gath_ps", "gath_a", "gath_d"))
        split_free, w_hi_ok, w_lo_ok = (sem(n) for n in ("split_free", "w_hi_ok", "w_lo_ok"))
        g_ps, g_part, g_sum, u_ps, u_part, hid_ok, hidT_ps, hidT_hi, hidT_lo = (
            sem(n) for n in ("g_ps", "g_part", "g_sum", "u_ps", "u_part", "hid_ok", "hidT_ps", "hidT_hi", "hidT_lo"))
        y_ps, y_part_ok, y_free, y_st, ysb_free = (
            sem(n) for n in ("y_ps", "y_part_ok", "y_free", "y_st", "ysb_free"))
        fetch = [sem(f"fetch{i}") for i in range(4)]
        held = sem("held")
        pick_ok, rows_ok, ysb_ld, ysb_used = (sem(n) for n in ("pick_ok", "rows_ok", "ysb_ld", "ysb_used"))
        fin_c, res_ok, ssq3, var3, std3, inv3, fin_s, fin_ok, out_st = (
            sem(n) for n in ("fin_c", "res_ok", "ssq3", "var3", "std3", "inv3", "fin_s", "fin_ok", "out_st"))

        units = pair_units()

        def unit_count(s, u):
            return (s * (PAIR_UNITS // RING) + (MIX_UNITS // RING + u // RING + 1)) * 16

        def more_passes(eng, body, between=None):
            eng.wait_ge(route_ok, 1)
            most = eng.value_load(count[0:1, 0:1], min_val=0, max_val=TOK)
            with eng.If(most > CAP):
                with eng.Fori(0, PASSES - 1) as r:
                    if between:
                        between(r)
                    with eng.Fori(0, PAIRS) as q:
                        body(r * PAIRS + q + PAIRS, q)

        block = ctx.enter_context(nc.Block())

        @block.sync
        def _(sp):
            sp.dma_start(x_in[:], t["x"].rearrange("(t p) d -> p t d", p=P)).then_inc(x_ld, 16)

            def load(slot, src, cols):
                sp.dma_start(ring[:, slot, :].rearrange("p (k n) -> p k n", n=cols), src).then_inc(landed[slot], 16)

            def rows4(w, j, c0):
                return w[j * 512:(j + 1) * 512, bass.ds(c0, BLK)].rearrange("(t p) n -> p t n", p=P)

            for j in range(RING):
                load(j, rows4(t["w_in"], j, 0), BLK)
            with sp.Fori(1, 4) as b:
                for j in range(4):
                    sp.wait_ge(unit_free, b * 4 + (j - 3))
                    load(j, rows4(t["w_in"], j, b * BLK), BLK)
            with sp.Fori(0, 4) as b:
                for j in range(4):
                    sp.wait_ge(unit_free, b * 4 + (16 + j - 3))
                    load(j, rows4(t["w_gate"], j, b * BLK), BLK)
            u = 32
            for w, nblk, nj in (("w_up_pool", 2, 2), ("w_up_attn", 2, 2), ("w_out", 2, 4)):
                for b in range(nblk):
                    for j in range(nj):
                        sp.wait_ge(unit_free, u - 3)
                        load(u % RING, rows4(t[w], j, b * BLK), BLK)
                        u += 1

            def pair(step, q):
                for u, (kind, e, half) in enumerate(units):
                    sp.wait_ge(unit_free, step * PAIR_UNITS + (MIX_UNITS + u - 3))
                    expert = bass.ds(q * 2 + e, 1)
                    if kind == "down":
                        src = t["w_e_down"][expert, :, half * BLK:(half + 1) * BLK].rearrange(
                            "e (k p) n -> p (e k) n", p=P)
                        load(u % RING, src, BLK)
                    else:
                        src = t["w_e_" + kind][expert].rearrange("e (p k) n -> p (e k) n", p=P)
                        load(u % RING, src[:, half * 8:(half + 1) * 8, :], F_EXP)

            with sp.Fori(0, PAIRS) as s:
                pair(s, s)
            more_passes(sp, pair)
            for tt in range(TT):
                sp.wait_ge(fin_ok, tt + 1)
                sp.dma_start(t["out"][tt * P:(tt + 1) * P, :], h[:, tt, :]).then_inc(out_st, 16)
            sp.wait_ge(out_st, 16 * TT)

        @block.gpsimd
        def _(pool):
            pool.dma_start(pool_at[:], t["c_pool"].rearrange("(t p) g n -> p t g n", p=P)).then_inc(pool_ld, 16)
            pool.dma_start(w_mix[:], t["pool_mix"].rearrange("g (k p) n -> p (g k) n", p=P)).then_inc(pool_ld, 16)
            pool.dma_start(b_gate[:], t["b_gate"].partition_broadcast(P)).then_inc(bg_ld, 16)
            pool.dma_start(w_rout[:], t["w_rout"].rearrange("(k p) n -> p k n", p=P)).then_inc(rout_ld, 16)
            pool.dma_start(b_rout, t["b_rout"].partition_broadcast(P)).then_inc(rout_ld, 16)
            pool.dma_start(tri[:], t["c_tri"]).then_inc(rout_ld, 16)
            pool.dma_start(ones[:], t["c_ones"]).then_inc(rout_ld, 16)
            pool.dma_start(iota[:], t["c_iota"]).then_inc(rout_ld, 16)
            pool.wait_ge(bank7_free, HEADS + 1)
            pool.dma_start(gain_ffn[:], t["gain_ffn"].partition_broadcast(P)).then_inc(gffn_ld, 16)
            pool.dma_start(x_again[:], t["x"].rearrange("(t p) d -> p t d", p=P)).then_inc(x2_ld, 16)

            def pair(s, q):
                pool.wait_ge(y_free, s * 4 + 4)
                pool.dma_start(t["y_rows"][bass.ds(q * P, P), :], y_sb[:]).then_inc(y_st, 16)
                pool.wait_ge(y_st, s * 16 + 16)
                pool.sem_inc(ysb_free, 1)

            def row(tt, j):
                return bass.IndirectOffsetOnAxis(ap=rows[:, tt, j:j + 1], axis=0)

            def between(r):
                pool.wait_ge(pick_ok, r + 1)
                pool.sem_inc(held, 1)
                for i in range(2 * TT):
                    if i:
                        pool.wait_ge(ysb_used, r * (2 * TT) + i)
                        pool.sem_inc(held, 1)
                    pool.indirect_dma_start(y_sb[:], None, t["y_rows"], row(i // 2, i % 2)).then_inc(ysb_ld, 16)
                pool.wait_ge(ysb_ld, r * (32 * TT) + 32 * TT)
                pool.sem_inc(held, 1)

            with pool.Fori(0, PAIRS) as s:
                pair(s, s)
            more_passes(pool, pair, between)
            pool.wait_ge(rows_ok, 1)
            pool.dma_start(gain_out[:], t["gain_out"].partition_broadcast(P)).then_inc(gout_ld, 16)
            for tt in range(TT):
                for j in range(2):
                    pool.indirect_dma_start(fetched[:, tt, j, :], None, t["y_rows"],
                                            row(tt, j)).then_inc(fetch[2 * tt + j], 16)

        @block.tensor
        def _(pe):
            mm = nc.tensor.matmul

            pe.wait_ge(tab_ld, 48)
            pe.wait_ge(table_ok, 1)
            mm(bank[0:HEADS, 0, :], table[:], onehot[:], start=True, stop=True).then_inc(bias_row_ps, 1)
            pe.wait_ge(hankel_ld, 16)
            for i in range(4):
                mm(bank[:, 4 + i, :], flip[:], hankel[:, 2 * i:2 * i + 2, :], start=True, stop=True).then_inc(flip_ps, 1)

            def transposes(src, done):
                for f in range(8):
                    for i in range(2):
                        for tt in range(TT):
                            c = (2 * f + i) * P
                            last = nc.tensor.transpose(bank[:, f, i * TOK + tt * P:i * TOK + (tt + 1) * P],
                                                       src[:, tt, c:c + P], ident[:])
                    last.then_inc(done, 1)

            pe.wait_ge(bias_ok, 4)
            pe.wait_ge(id_ld, 16)
            pe.wait_ge(xs_ok, TT)
            transposes(x_in, xT_ps)
            pe.wait_ge(emptied_a, 4)
            pe.wait_ge(emptied_d, 4)

            def unit(slot, actT, k0, first, last, bank0, wait_bank=None):
                for k in range(4):
                    for c in range(2):
                        for tt in range(TT):
                            if wait_bank and first and k == 0:
                                wait_bank(2 * c + tt)
                            ins = mm(bank[:, bank0 + 2 * c + tt, :], actT[:, k0 + k, tt * P:(tt + 1) * P],
                                     ring[:, slot, k * BLK + c * BANK:k * BLK + (c + 1) * BANK],
                                     start=first and k == 0, stop=last and k == 3)
                ins.then_inc(unit_free, 1)

            with pe.Fori(0, 2) as b:
                for half in range(2):
                    pe.wait_ge(emptied_a, b * 4 + (2 * half + 2))
                    pe.wait_ge(emptied_d, b * 4 + (2 * half + 2))
                    for j in range(4):
                        pe.wait_ge(landed[j], b * 32 + 16 * (half + 1))
                        unit(j, xT, 4 * j, j == 0, j == 3, 4 * half)

            pe.wait_ge(pool_ld, 32)
            pe.wait_ge(emptied_a, 10)
            pe.wait_ge(emptied_d, 10)
            for c in range(8):
                g = c // 2
                for tt in range(TT):
                    last = mm(bank[:, c // 2, (c % 2) * TOK + tt * P:(c % 2 + 1) * TOK],
                              proj[:, tt, c * P:(c + 1) * P], pool_at[:, tt, g, tt * P:TOK],
                              start=tt == 0, stop=tt == TT - 1)
                if c % 2:
                    last.then_inc(pooled_ps, 1)
            pe.wait_ge(low_free, 4)
            pe.wait_ge(emptied_a, 12)
            pe.wait_ge(emptied_d, 12)
            for g in range(4):
                for m in range(2):
                    for k in range(2):
                        last = mm(bank[:, 4 + g, m * TOK:(m + 1) * TOK], w_mix[:, 2 * g + k, m * P:(m + 1) * P],
                                  pooledT[:, 2 * g + k, :], start=k == 0, stop=k == 1)
                last.then_inc(mixed_ps, 1)

            def head_transpose(n):
                pe.wait_ge(staged, n)
                for a in range(2):
                    for tt in range(TT):
                        last = nc.tensor.transpose(bank[:, 4, a * TOK + tt * P:a * TOK + (tt + 1) * P],
                                                   qk[:, a, tt, :], ident[:])
                last.then_inc(qkT_ps, 1)

            def head_scores(n):
                pe.wait_ge(qkT_ok, n)
                for c in range(2):
                    lanes = slice(DH * c, DH * c + DH)
                    mm(bank[:, 5 + c, 0:P], qkT[lanes, 0, 0:P], qkT[lanes, 1, 0:P], start=True, stop=True)
                    last = mm(bank[:, 5 + c, P:P + TOK], qkT[lanes, 0, P:TOK], qkT[lanes, 1, :], start=True, stop=True)
                last.then_inc(s_ps, 1)

            def head_map_transpose(n):
                pe.wait_ge(a_ok, n)
                pe.wait_ge(bank7_free, n)
                for i in range(3):
                    last = nc.tensor.transpose(bank[:, 7, i * P:(i + 1) * P], amap[:, i * P:(i + 1) * P], ident[:])
                last.then_inc(aT_ps, 1)

            def head_values(n, head):
                pe.wait_ge(aT_ok, n)
                v = [proj[:, tt, bass.ds(head * P + 3 * BLK, P)] for tt in range(TT)]
                mm(bank[:, 4, 0:P], amapT[:, 0:P], v[0], start=True, stop=True)
                mm(bank[:, 4, P:2 * P], amapT[:, P:2 * P], v[0], start=True, stop=False)
                mm(bank[:, 4, P:2 * P], amapT[:, 2 * P:3 * P], v[1], start=False, stop=True).then_inc(o_ps, 1)

            def head_out_transpose(n):
                pe.wait_ge(on_ok, n)
                for tt in range(TT):
                    last = nc.tensor.transpose(bank[:, 7, tt * P:(tt + 1) * P], o_n[:, tt, :], ident[:])
                last.then_inc(oT_ps, 1)

            with pe.Fori(0, 4) as b:
                for j in range(4):
                    pe.wait_ge(landed[j], b * 16 + 80)
                    n = b * 2 + (j // 2 + 1)
                    for k in range(4):
                        point = 4 * (j % 2) + k
                        if point == 0:
                            head_transpose(n)
                        if point == 1:
                            head_scores(n)
                        if point == 4:
                            head_map_transpose(n)
                        if point == 5:
                            head_values(n, b * 2 + j // 2)
                        if point == 7:
                            head_out_transpose(n)
                        for c in range(2):
                            for tt in range(TT):
                                if j == 0 and k == 0:
                                    pe.wait_ge(low_free, b * 4 + (2 * c + tt + 1))
                                ins = mm(bank[:, 2 * c + tt, :], xT[:, 4 * j + k, tt * P:(tt + 1) * P],
                                         ring[:, j, k * BLK + c * BANK:k * BLK + (c + 1) * BANK],
                                         start=j == 0 and k == 0, stop=j == 3 and k == 3)
                    ins.then_inc(unit_free, 1)

            u = 32
            for b in range(4):
                if b == 0:
                    pe.wait_ge(low_free, 20)
                if b == 1:
                    pe.wait_ge(bank7_free, HEADS + 1)
                for j in range(2):
                    pe.wait_ge(landed[u % RING], 16 * (u // RING + 1))
                    unit(u % RING, mixedT if b < 2 else oT, 4 * j, j == 0, j == 1, 4 * (b % 2),
                         (lambda k: pe.wait_ge(up_free, 4 * (b - 2) + k + 1)) if b >= 2 else None)
                    u += 1

            for half in range(2):
                pe.wait_ge(merged_ok, half + 1)
                for f in range(4 * half, 4 * half + 4):
                    for i in range(2):
                        for tt in range(TT):
                            c = (2 * f + i) * P
                            last = nc.tensor.transpose(bank[:, f, i * TOK + tt * P:i * TOK + (tt + 1) * P],
                                                       merged[:, tt, c:c + P], ident[:])
                    last.then_inc(mT_ps, 1)
            pe.wait_ge(mT_a, 4)
            pe.wait_ge(mT_d, 4)
            for b in range(2):
                for j in range(4):
                    pe.wait_ge(landed[u % RING], 16 * (u // RING + 1))
                    unit(u % RING, mergedT, 4 * j, j == 0, j == 3, 4 * b)
                    u += 1

            pe.wait_ge(hn_ok, TT)
            transposes(hn, hnT_ps)
            pe.wait_ge(hnT_a, 4)
            pe.wait_ge(hnT_d, 4)
            pe.wait_ge(rout_ld, 80)
            for tt in range(TT):
                for k in range(KT):
                    last = mm(bank[:, 0, tt * 64:tt * 64 + 36], hnT[:, k, tt * P:(tt + 1) * P], w_rout[:, k, :],
                              start=k == 0, stop=k == KT - 1)
            last.then_inc(logit_ps, 1)
            pe.wait_ge(mask_ok, 1)
            mask = rt[:, :, 6, 0:32]
            mm(bank[:, 1, 0:32], tri[:], mask[:, 0, :], start=True, stop=True)
            mm(bank[:, 1, 32:64], ones[:], mask[:, 0, :], start=True, stop=False)
            mm(bank[:, 1, 32:64], tri[:], mask[:, 1, :], start=False, stop=True)
            mm(bank[:, 1, 64:96], ones[:], mask[:, 0, :], start=True, stop=False)
            mm(bank[:, 1, 64:96], ones[:], mask[:, 1, :], start=False, stop=True).then_inc(rank_ps, 1)

            def gather_fill(f):
                for part_i, src in enumerate((hn_hi, hn_lo)):
                    for i in range(2):
                        c = part_i * 256 + i * P
                        for tt in range(TT):
                            last = mm(bank[:, 7, c:c + P], src[:, tt, 2 * f + i, :], sel[:, tt, :],
                                      start=tt == 0, stop=tt == TT - 1)
                last.then_inc(gath_ps, 1)

            pe.wait_ge(lo_ok, TT)
            pe.wait_ge(sel_ok, 1)
            for f in range(FILLS):
                if f % 2:
                    pe.wait_ge(gath_a, (f + 1) // 2)
                elif f:
                    pe.wait_ge(gath_d, f // 2)
                gather_fill(f)
            pe.sem_inc(split_free, NQ)

            def pair(s, _):
                for u, (kind, e, half) in enumerate(units):
                    slot = u % RING
                    if u == 0:
                        pe.wait_ge(gath_a, s * 4 + 4)
                        pe.wait_ge(gath_d, s * 4 + 4)
                    if u == 8:
                        pe.wait_ge(hidT_lo, s * 2 + 1)
                        pe.wait_ge(sel_ok, s + 2)
                    if u == 10:
                        pe.wait_ge(hidT_lo, s * 2 + 2)
                    if u >= 10:
                        pe.wait_ge(y_free, s * 4 + (u - 9))
                    if u >= 8:
                        f = 2 * (u - 8)
                        pe.wait_ge(gath_d, s * 4 + (4 + f // 2))
                        gather_fill(f)
                    pe.wait_ge(landed[slot], unit_count(s, u))

                    def tile(i, moving_hi, moving_lo):
                        if kind == "down":
                            k, c = i // 2, i % 2
                            stat_op, out = hidT[:, e, k, :], bank[:, 2 + 2 * half + c, :]
                            head, tail = k == 0, k == 3
                        else:
                            k = 8 * half + i
                            stat_op, out = xg[:, 2 * k + e, :, :], bank[:, 0 if kind == "gate" else 1, :]
                            head, tail = k == 0, k == KT - 1
                        if moving_hi is None:
                            return mm(out, stat_op.bitcast(F32), ring[:, slot, i * BANK:(i + 1) * BANK],
                                      start=head, stop=tail)
                        mm(out, stat_op, moving_hi, start=head, stop=False)
                        return mm(out, stat_op, moving_lo, start=False, stop=tail)

                    for g in range(NG):
                        n = s * (PAIR_UNITS * NG) + (u * NG + g + 1)
                        b = (u * NG + g) % NQ
                        pe.wait_ge(w_lo_ok, n)
                        for i in range(2):
                            last = tile(2 * g + i, w_hi[:, b, i * BANK:(i + 1) * BANK], w_lo[:, b, i * BANK:(i + 1) * BANK])
                        last.then_inc(split_free, 1)
                    if u >= 8:
                        f = 2 * (u - 8) + 1
                        pe.wait_ge(gath_a, s * 4 + (4 + (f + 1) // 2))
                        gather_fill(f)
                    for i in range(2 * NG, 8):
                        if i == 7 and u in (4, 8):
                            pe.wait_ge(hid_ok, s * 2 + (u // 4))
                        last = tile(i, None, None)
                    last.then_inc(unit_free, 1)
                    if u in (4, 8):
                        for k in range(4):
                            last = nc.tensor.transpose(bank[:, 6, k * CAP:(k + 1) * CAP], hid[:, k * P:(k + 1) * P],
                                                       ident[0:CAP, 0:CAP])
                        last.then_inc(hidT_ps, 1)

            with pe.Fori(0, PAIRS) as s:
                pair(s, s)
            more_passes(pe, pair)

        @block.scalar
        def _(act):
            f = nc.scalar.activation
            act.dma_start(table[0:32, :], t["table"]).then_inc(tab_ld, 16)
            act.dma_start(onehot[:], t["c_onehot"]).then_inc(tab_ld, 16)
            act.dma_start(flip[:], t["c_flip"]).then_inc(tab_ld, 16)
            act.dma_start(ident[:], t["c_eye"]).then_inc(id_ld, 16)
            act.dma_start(gain_mix, t["gain_mix"]).then_inc(sm_ld, 16)
            act.dma_start(pool_scale, t["pool_scale"]).then_inc(sm_ld, 16)
            act.dma_start(subln, t["subln"]).then_inc(sm_ld, 16)
            act.dma_start(lam_in[:], t["lam"].partition_broadcast(P)).then_inc(lam_ld, 16)

            act.wait_ge(bias_row_ps, 1)
            f(bias_rows[:], bank[0:HEADS, 0, :], ACT.Copy).then_inc(bias_row_sb, 1)
            act.wait_ge(bias_row_sb, 1)
            act.dma_start(t["bias_dram"], bias_rows[:]).then_inc(bias_st, 16)
            act.wait_ge(bias_st, 16)
            src = bass.AP(tensor=t["bias_dram"].tensor, offset=t["bias_dram"].offset, ap=[[1, P], [BANK, HEADS], [1, 256]])
            act.dma_start(hankel[:], src).then_inc(hankel_ld, 16)

            act.wait_ge(x_ld, 16)
            for tt in range(TT):
                f(xT[:, 8 * tt:8 * tt + 8, :].rearrange("p k n -> p (k n)"), x_in[:, tt, :], ACT.Square,
                  accum_out=stat[:, tt:tt + 1]).then_inc(ssq1, 1)
            act.wait_ge(var1, 1)
            f(stat[:, 4:6], stat[:, 2:4], ACT.Sqrt).then_inc(std1, 1)
            act.wait_ge(inv1, 1)
            for tt in range(TT):
                f(x_in[:, tt, :], x_in[:, tt, :], ACT.Copy, scale=stat[:, 6 + tt:7 + tt]).then_inc(xs_ok, 1)
            act.wait_ge(sm_ld, 48)
            for b in (0, 1, 4, 5):
                act.wait_ge(xT_ps, b + 1)
                for i in range(2):
                    last = f(xT[:, 2 * b + i, :], bank[:, b, i * TOK:(i + 1) * TOK], ACT.Copy,
                             scale=gain_mix[:, 2 * b + i:2 * b + i + 1])
                last.then_inc(emptied_a, 1)
            act.wait_ge(lam_dot, 1)
            f(lam_s[:, 2:4], lam_s[:, 0:2], ACT.Exp).then_inc(lam_exp, 1)

            with act.Fori(0, 2) as b:
                for half in range(2):
                    act.wait_ge(unit_free, b * 8 + 4 * (half + 1))
                    for tt in range(TT):
                        f(proj[:, tt, bass.ds(b * (2 * BLK) + half * BLK, BANK)], bank[:, 4 * half + tt, :],
                          ACT.Copy).then_inc(emptied_a, 1)
            for g in range(4):
                act.wait_ge(mixed_ps, g + 1)
                for m in range(2):
                    c = 2 * g + m
                    last = f(mixedT[:, c, :], bank[:, 4 + g, m * TOK:(m + 1) * TOK], ACT.Copy,
                             scale=pool_scale[:, c:c + 1])
            last.then_inc(bank7_free, 1)
            act.wait_ge(emptied_d, 12)
            act.wait_ge(emptied_a, 12)

            def stage(n, head):
                for a, scale in ((0, float(DH) ** -0.5), (1, 1.0)):
                    last = f(qk[:, a, :, :], proj[:, :, bass.ds(head * P + (1 + a) * BLK, P)], ACT.Copy, scale=scale)
                last.then_inc(staged, 1)

            with act.Fori(0, 4) as b:
                for hh in range(2):
                    n, head = b * 2 + (hh + 1), b * 2 + hh
                    stage(n, head)
                    act.wait_ge(qkT_ps, n)
                    f(qkT[:].rearrange("p a n -> p (a n)"), bank[:, 4, :], ACT.Copy).then_inc(qkT_ok, 1)
                    act.wait_ge(nmax_ok, n)
                    for qt, (lo, hi) in enumerate(((0, P), (P, 3 * P))):
                        for c in range(2):
                            i = 2 * qt + c
                            last = f(probs[:, c, lo:hi], probs[:, c, lo:hi], ACT.Exp, bias=nmax[:, i:i + 1],
                                     accum_out=sums[:, i:i + 1])
                    last.then_inc(p_ok, 1)
                    act.wait_ge(aT_ps, n)
                    f(amapT[:], bank[:, 7, 0:3 * P], ACT.Copy).then_inc(aT_ok, 1)
                    act.wait_ge(o_ps, n)
                    for tt in range(TT):
                        last = f(o_sq[:, tt, :], bank[:, 4, tt * P:(tt + 1) * P], ACT.Square,
                                 accum_out=ssq_o[:, tt:tt + 1])
                    last.then_inc(ssq_ok, 1)
                    act.wait_ge(var_ok, n)
                    f(std_o, var_o, ACT.Sqrt).then_inc(std_ok, 1)
                    act.wait_ge(oT_ps, n)
                    f(oT[:, bass.ds(head, 1), :].rearrange("p a n -> p (a n)"), bank[:, 7, 0:TOK], ACT.Copy,
                      scale=gain_o).then_inc(bank7_free, 1)
                act.wait_ge(low_free, b * 4 + 8)
                cols = bass.ds(b * BLK, BLK)
                f(gates[:, :, cols], gates[:, :, cols], ACT.Sigmoid).then_inc(sig_ok, 1)

            def copy_banks(ps, dst, done):
                for b in (0, 1, 4, 5):
                    act.wait_ge(ps, b + 1)
                    f(dst[:, 2 * b:2 * b + 2, :].rearrange("p k n -> p (k n)"), bank[:, b, :], ACT.Copy).then_inc(done, 1)

            copy_banks(mT_ps, mergedT, mT_a)

            for tt in range(TT):
                act.wait_ge(h_ok, 6 + tt)
                if tt == 0:
                    act.wait_ge(h_ok, 8)
                f(hn[:, tt, :], h[:, tt, :], ACT.Square, accum_out=stat[:, 8 + tt:9 + tt]).then_inc(ssq2, 1)
            act.wait_ge(var2, 1)
            f(stat[:, 12:14], stat[:, 10:12], ACT.Sqrt).then_inc(std2, 1)
            act.wait_ge(inv2, 1)
            act.wait_ge(ssq2, TT)
            for tt in range(TT):
                f(hn[:, tt, :], h[:, tt, :], ACT.Copy, scale=stat[:, 14 + tt:15 + tt]).then_inc(hs_ok, 1)
            copy_banks(hnT_ps, hnT, hnT_a)
            act.wait_ge(hn_ok, TT)
            for tt in range(TT):
                f(hn_hi[:, tt, :, :], hn[:, tt, :].rearrange("p (q k) -> p k q", k=KT), ACT.Copy).then_inc(hi_ok, 1)
            act.wait_ge(gdiff, 1)
            f(rt[:, :, 1, 0:4], rt[:, :, 1, 0:4], ACT.Exp).then_inc(gexp, 1)
            act.wait_ge(mdiff, 1)
            f(stat[:, 20:22], stat[:, 18:20], ACT.Exp).then_inc(mexp, 1)

            def gather_out(f_i, n):
                act.wait_ge(gath_ps, n)
                src = bank[:, 7, :].rearrange("p (a c s) -> p a c s", a=2, s=CAP)
                f(xg[:, 4 * f_i:4 * f_i + 4, :, :].rearrange("p c a s -> p a c s"), src, ACT.Copy).then_inc(gath_a, 1)

            for f_i in range(0, FILLS, 2):
                gather_out(f_i, f_i + 1)

            def pair(s, q):
                def after(u):
                    kind, e, half = units[u]
                    n = s * 2 + (e + 1)
                    done = s * PAIR_UNITS + (MIX_UNITS + u + 1)
                    if kind == "gate" and half == 1:
                        act.wait_ge(unit_free, done)
                        f(part[:], bank[CAP:P, 0, :], ACT.Copy).then_inc(g_part, 1)
                    if kind == "up" and half == 1:
                        act.wait_ge(g_sum, n)
                        f(silu_g[:], g_sb[:], ACT.Silu)
                        act.wait_ge(unit_free, done)
                        f(part[:], bank[CAP:P, 1, :], ACT.Copy).then_inc(u_part, 1)
                    if u in (4, 8):
                        act.wait_ge(hidT_ps, s * 2 + (u // 4))
                        f(hidT[:, u // 4 - 1, :, 0:CAP], bank[:, 6, 0:4 * CAP].rearrange("p (k s) -> p k s", s=CAP),
                          ACT.Copy).then_inc(hidT_hi, 1)
                    if kind == "down":
                        act.wait_ge(unit_free, done)
                        if u > 8:
                            act.wait_ge(y_free, s * 4 + (u - 8))
                        f(y_part[:], bank[CAP:P, 2 + 2 * half:4 + 2 * half, :].rearrange("p b n -> p (b n)"),
                          ACT.Copy).then_inc(y_part_ok, 1)

                for u in range(PAIR_UNITS):
                    act.wait_ge(landed[u % RING], unit_count(s, u))
                    for g in range(NG):
                        b = (u * NG + g) % NQ
                        act.wait_ge(split_free, s * (PAIR_UNITS * NG) + (u * NG + g + 1))
                        f(w_hi[:, b, :], ring[:, u % RING, g * 1024:(g + 1) * 1024], ACT.Copy).then_inc(w_hi_ok, 1)
                    if u >= 8:
                        f_i = 2 * (u - 8)
                        gather_out(f_i, s * FILLS + (FILLS + f_i + 1))
                    if u:
                        after(u - 1)
                after(PAIR_UNITS - 1)

            with act.Fori(0, PAIRS) as s:
                pair(s, s)
            more_passes(act, pair)

            for tt in range(TT):
                act.wait_ge(res_ok, tt + 1)
                f(fetched[:, tt, 0, :], h[:, tt, :], ACT.Square, accum_out=stat[:, 24 + tt:25 + tt]).then_inc(ssq3, 1)
            act.wait_ge(var3, 1)
            f(stat[:, 28:30], stat[:, 26:28], ACT.Sqrt).then_inc(std3, 1)
            act.wait_ge(inv3, 1)
            for tt in range(TT):
                f(h[:, tt, :], h[:, tt, :], ACT.Copy, scale=stat[:, 30 + tt:31 + tt]).then_inc(fin_s, 1)

        @block.vector
        def _(dve):
            v = nc.vector
            chain = Chain(dve, dve_c)

            def step(ins):
                chain.step(ins)
                chain.settle()

            v.memset(table[32:33, :], NEG).then_inc(table_ok, 1)

            def inverse_rms(ssq_sem, c, var_sem, std_sem, inv_sem, width, n):
                dve.wait_ge(ssq_sem, n)
                v.tensor_scalar(stat[:, c + 2:c + 4], stat[:, c:c + 2], 1.0 / width, EPS, ALU.mult, ALU.add).then_inc(var_sem, 1)
                dve.wait_ge(std_sem, 1)
                v.reciprocal(stat[:, c + 6:c + 8], stat[:, c + 4:c + 6]).then_inc(inv_sem, 1)

            for i in range(4):
                dve.wait_ge(flip_ps, i + 1)
                src = bank[:, 4 + i, :].rearrange("p (a n) -> p a n", a=2)
                v.tensor_copy(bias[:, 2 * i:2 * i + 2, P:3 * P], src)
                v.tensor_copy(bias[:, 2 * i:2 * i + 2, 0:P], src[:, :, P:2 * P]).then_inc(bias_ok, 1)
            inverse_rms(ssq1, 0, var1, std1, inv1, D, TT)
            dve.wait_ge(sm_ld, 48)
            step(v.tensor_scalar(gain_o, subln, 1.0 - LAMBDA_INIT, None, ALU.mult))
            dve.wait_ge(lam_ld, 16)
            lam_v = lam_in[:].rearrange("p (a b) n -> p a b n", b=2)
            step(v.tensor_tensor(lam_prod[:], lam_v[:, :, 0, :], lam_v[:, :, 1, :], ALU.mult))
            v.tensor_reduce(lam_s[:, 0:2], lam_prod[:], AX, ALU.add).then_inc(lam_dot, 1)
            for b in (2, 3, 6, 7):
                dve.wait_ge(xT_ps, b + 1)
                for i in range(2):
                    last = v.tensor_scalar(xT[:, 2 * b + i, :], bank[:, b, i * TOK:(i + 1) * TOK],
                                           gain_mix[:, 2 * b + i:2 * b + i + 1], None, ALU.mult)
                last.then_inc(emptied_d, 1)
            dve.wait_ge(lam_exp, 1)
            step(v.tensor_tensor(lam_s[:, 4:5], lam_s[:, 3:4], lam_s[:, 2:3], ALU.subtract))
            step(v.tensor_scalar(nlam, lam_s[:, 4:5], -LAMBDA_INIT, None, ALU.add))

            with dve.Fori(0, 2) as b:
                for half in range(2):
                    dve.wait_ge(unit_free, b * 8 + 4 * (half + 1))
                    for tt in range(TT):
                        v.tensor_copy(proj[:, tt, bass.ds(b * (2 * BLK) + (half * BLK + BANK), BANK)],
                                      bank[:, 4 * half + 2 + tt, :]).then_inc(emptied_d, 1)
            for b in range(4):
                dve.wait_ge(pooled_ps, b + 1)
                v.tensor_copy(pooledT[:, 2 * b:2 * b + 2, :].rearrange("p k n -> p (k n)"), bank[:, b, :]).then_inc(low_free, 1)
            dve.wait_ge(bg_ld, 16)

            with dve.Fori(0, 4) as b:
                chain.enter(b, 10)
                for hh in range(2):
                    n, head = b * 2 + (hh + 1), b * 2 + hh
                    dve.wait_ge(s_ps, n)
                    v.tensor_tensor(probs[:], bank[:, 5:7, 0:3 * P],
                                    bias[:, bass.ds(head, 1), :].to_broadcast([P, 2, 3 * P]), ALU.add).then_inc(s_free, 1)
                    dve.wait_ge(s_free, n)
                    v.tensor_reduce(nmax[:, 0:2], probs[:, :, 0:P], AX, ALU.max, negate=True)
                    v.tensor_reduce(nmax[:, 2:4], probs[:, :, P:3 * P], AX, ALU.max, negate=True).then_inc(nmax_ok, 1)
                    dve.wait_ge(p_ok, n)
                    step(v.reciprocal(inv, sums))
                    step(v.tensor_scalar(coef, inv.rearrange("p (q c) -> p q c", c=2)[:, :, 1], nlam, None, ALU.mult))
                    chain.step(v.tensor_scalar(amap[:, 0:P], probs[:, 1, 0:P], coef[:, 0:1], None, ALU.mult))
                    step(v.tensor_scalar(amap[:, P:3 * P], probs[:, 1, P:3 * P], coef[:, 1:2], None, ALU.mult))
                    v.scalar_tensor_tensor(out=amap[:, 0:P], in0=probs[:, 0, 0:P], scalar=inv[:, 0:1],
                                           in1=amap[:, 0:P], op0=ALU.mult, op1=ALU.add)
                    v.scalar_tensor_tensor(out=amap[:, P:3 * P], in0=probs[:, 0, P:3 * P], scalar=inv[:, 2:3],
                                           in1=amap[:, P:3 * P], op0=ALU.mult, op1=ALU.add).then_inc(a_ok, 1)
                    dve.wait_ge(ssq_ok, n)
                    v.tensor_scalar(var_o, ssq_o, 1.0 / P, EPS, ALU.mult, ALU.add).then_inc(var_ok, 1)
                    dve.wait_ge(std_ok, n)
                    step(v.reciprocal(inv_o, std_o))
                    for tt in range(TT):
                        last = v.tensor_scalar(o_n[:, tt, :], bank[:, 4, tt * P:(tt + 1) * P], inv_o[:, tt:tt + 1],
                                               None, ALU.mult)
                    last.then_inc(on_ok, 1)
                dve.wait_ge(unit_free, b * 4 + 20)
                for c in range(2):
                    for tt in range(TT):
                        cols = bass.ds(b * BLK + c * BANK, BANK)
                        v.tensor_tensor(gates[:, tt, cols], bank[:, 2 * c + tt, :], b_gate[:, cols], ALU.add).then_inc(low_free, 1)
            chain.leave(4)

            for b in range(4):
                dve.wait_ge(sig_ok, 4)
                dve.wait_ge(unit_free, 32 + 2 * (b + 1))
                if b == 0:
                    dve.wait_ge(bank7_free, HEADS + 1)
                for c in range(2):
                    for tt in range(TT):
                        col = (b % 2) * BLK + c * BANK
                        src = bank[:, 4 * (b % 2) + 2 * c + tt, :]
                        dst = merged[:, tt, col:col + BANK]
                        if b < 2:
                            v.tensor_tensor(dst, src, gates[:, tt, col:col + BANK], ALU.mult).then_inc(up_free, 1)
                        else:
                            gate = gates[:, tt, D + col:D + col + BANK]
                            v.tensor_tensor(gate, src, gate, ALU.mult).then_inc(up_free, 1)
                if b >= 2:
                    dve.wait_ge(up_free, 4 * (b + 1))
                    for tt in range(TT):
                        col = (b % 2) * BLK
                        dst = merged[:, tt, col:col + BLK]
                        last = v.tensor_tensor(dst, dst, gates[:, tt, D + col:D + col + BLK], ALU.add)
                    last.then_inc(merged_ok, 1)

            def copy_banks(ps, dst, done):
                for b in (2, 3, 6, 7):
                    dve.wait_ge(ps, b + 1)
                    v.tensor_copy(dst[:, 2 * b:2 * b + 2, :].rearrange("p k n -> p (k n)"), bank[:, b, :]).then_inc(done, 1)

            copy_banks(mT_ps, mergedT, mT_d)
            dve.wait_ge(x2_ld, 16)
            for b in range(2):
                dve.wait_ge(unit_free, 40 + 4 * (b + 1))
                for tt in range(TT):
                    for c in range(2):
                        col = b * BLK + c * BANK
                        v.tensor_tensor(h[:, tt, col:col + BANK], bank[:, 4 * b + 2 * c + tt, :],
                                        x_again[:, tt, col:col + BANK], ALU.add).then_inc(h_ok, 1)
            inverse_rms(ssq2, 8, var2, std2, inv2, D, TT)
            dve.wait_ge(gffn_ld, 16)
            for tt in range(TT):
                dve.wait_ge(hs_ok, tt + 1)
                v.tensor_tensor(hn[:, tt, :], hn[:, tt, :], gain_ffn[:], ALU.mult).then_inc(hn_ok, 1)
            copy_banks(hnT_ps, hnT, hnT_d)

            dve.wait_ge(logit_ps, 1)
            logits = rt[:, :, 0, 0:36]
            step(v.tensor_tensor(logits, bank[:, 0, 0:128].rearrange("p (t n) -> p t n", t=TT)[:, :, 0:36],
                                 b_rout.rearrange("p (a n) -> p a n", a=1).to_broadcast([P, TT, 36]), ALU.add))

            def wide(x, n):
                return x.rearrange("p (t a) -> p t a", a=1).to_broadcast([P, TT, n])

            def first_of(vals, top, n, tmp, idx, hot):
                step(v.tensor_reduce(top, vals, AX, ALU.max))
                step(v.tensor_tensor(tmp, vals, wide(top, n), ALU.is_equal))
                cols = iota[:, 0:n].rearrange("p (a n) -> p a n", a=1).to_broadcast([P, TT, n])
                step(v.scalar_tensor_tensor(out=tmp, in0=tmp, scalar=-BIG, in1=cols, op0=ALU.mult, op1=ALU.add))
                step(v.tensor_reduce(idx, tmp, AX, ALU.min))
                step(v.tensor_tensor(hot, tmp, wide(idx, n), ALU.is_equal))

            gtop, gidx = stat[:, 0:2], stat[:, 2:4]
            top1, idx1, top2, idx2 = stat[:, 4:6], stat[:, 6:8], stat[:, 14:16], stat[:, 16:18]
            ghot = rt[:, :, 2, 0:4]
            first_of(rt[:, :, 0, 0:4], gtop, 4, rt[:, :, 1, 0:4], gidx, ghot)
            v.tensor_tensor(rt[:, :, 1, 0:4], rt[:, :, 0, 0:4], wide(gtop, 4), ALU.subtract).then_inc(gdiff, 1)
            step(v.tensor_scalar(ghot, ghot, -NEG, NEG, ALU.mult, ALU.add))
            elog = rt[:, :, 3, 0:32]
            for tt in range(TT):
                ins = v.tensor_tensor(rt[:, tt, 3, 0:32].rearrange("p (g e) -> p g e", g=N_GROUPS),
                                      rt[:, tt, 0, 4:36].rearrange("p (g e) -> p g e", g=N_GROUPS),
                                      rt[:, tt, 2, 0:4].rearrange("p (g a) -> p g a", a=1).to_broadcast([P, N_GROUPS, 8]),
                                      ALU.add)
                chain.step(ins)
            chain.settle()
            hot1, hot2, both, tmp = rt[:, :, 4, 0:32], rt[:, :, 5, 0:32], rt[:, :, 6, 0:32], rt[:, :, 7, 0:32]
            first_of(elog, top1, 32, tmp, idx1, hot1)
            step(v.scalar_tensor_tensor(out=elog, in0=hot1, scalar=3 * NEG, in1=elog, op0=ALU.mult, op1=ALU.add))
            first_of(elog, top2, 32, tmp, idx2, hot2)
            v.tensor_tensor(both, hot1, hot2, ALU.add).then_inc(mask_ok, 1)
            v.tensor_tensor(stat[:, 18:20], top2, top1, ALU.subtract).then_inc(mdiff, 1)
            dve.wait_ge(gexp, 1)
            step(v.tensor_reduce(stat[:, 22:24], rt[:, :, 1, 0:4], AX, ALU.add))
            step(v.reciprocal(stat[:, 22:24], stat[:, 22:24]))
            dve.wait_ge(mexp, 1)
            step(v.tensor_scalar(stat[:, 24:26], stat[:, 20:22], 1.0, None, ALU.add))
            step(v.reciprocal(stat[:, 24:26], stat[:, 24:26]))
            step(v.tensor_tensor(topw[:, :, 0], stat[:, 24:26], stat[:, 22:24], ALU.mult))
            step(v.tensor_tensor(topw[:, :, 1], topw[:, :, 0], stat[:, 20:22], ALU.mult))
            dve.wait_ge(rank_ps, 1)
            rank_all = bank[:, 1, 0:64].rearrange("p (t e) -> p t e", t=TT)
            step(v.tensor_reduce(stat[:, 26:27], bank[:, 1, 64:96], AX, ALU.max))
            step(v.tensor_copy(count[:], stat[:, 26:27]))
            for j, (hot, idx) in enumerate(((hot1, idx1), (hot2, idx2))):
                step(v.tensor_tensor(tmp, rank_all, hot, ALU.mult))
                rank, steps = stat[:, 27:29], stat[:, 29:31]
                step(v.tensor_reduce(rank, tmp, AX, ALU.add))
                step(v.tensor_scalar(code[:, :, j], idx, BIG, float(CAP), ALU.add, ALU.mult))
                step(v.tensor_tensor(code[:, :, j], code[:, :, j], rank, ALU.add))
                for p in range(1, PASSES):
                    step(v.tensor_scalar(steps, rank, float(p * CAP), float(PAIRS * P - CAP), ALU.is_ge, ALU.mult))
                    step(v.tensor_tensor(code[:, :, j], code[:, :, j], steps, ALU.add))

            def one_hot():
                for tt in range(TT):
                    last = v.tensor_scalar(sel_a[:, tt, :], iota[:], code[:, tt, 0:1], None, ALU.is_equal)
                step(last)
                for tt in range(TT):
                    last = v.scalar_tensor_tensor(out=sel[:, tt, :], in0=iota[:], scalar=code[:, tt, 1:2],
                                                  in1=sel_a[:, tt, :], op0=ALU.is_equal, op1=ALU.add)
                last.then_inc(sel_ok, 1)

            one_hot()
            for tt in range(TT):
                dve.wait_ge(hi_ok, tt + 1)
                v.tensor_tensor(hn_lo[:, tt, :, :], hn[:, tt, :].rearrange("p (q k) -> p k q", k=KT),
                                hn_hi[:, tt, :, :].bitcast(F32), ALU.subtract).then_inc(lo_ok, 1)

            def gather_out(f_i, n):
                dve.wait_ge(gath_ps, n)
                src = bank[:, 7, :].rearrange("p (a c s) -> p a c s", a=2, s=CAP)
                v.tensor_copy(xg[:, 4 * f_i:4 * f_i + 4, :, :].rearrange("p c a s -> p a c s"), src).then_inc(gath_d, 1)

            for f_i in range(1, FILLS, 2):
                gather_out(f_i, f_i + 1)
            dve.wait_ge(gath_d, 4)
            dve.sem_inc(route_ok, 1)
            dve.sem_inc(ysb_free, 1)

            STEPS = 4

            def pair(s, q):
                chain.enter(q, STEPS)

                def after(u):
                    kind, e, half = units[u]
                    n = s * 2 + (e + 1)
                    if kind == "gate" and half == 1:
                        dve.wait_ge(g_part, n)
                        v.tensor_tensor(g_sb[:], bank[0:CAP, 0, :], part[:], ALU.add).then_inc(g_sum, 1)
                    if kind == "up" and half == 1:
                        dve.wait_ge(u_part, n)
                        step(v.tensor_tensor(u_sb[:], bank[0:CAP, 1, :], part[:], ALU.add))
                        v.tensor_tensor(hid[:], silu_g[:], u_sb[:], ALU.mult).then_inc(hid_ok, 1)
                    if u in (4, 8):
                        dve.wait_ge(hidT_hi, s * 2 + (u // 4))
                        e_t = u // 4 - 1
                        v.tensor_tensor(hidT[:, e_t, :, CAP:P], bank[:, 6, 0:4 * CAP].rearrange("p (k s) -> p k s", s=CAP),
                                        hidT[:, e_t, :, 0:CAP].bitcast(F32), ALU.subtract).then_inc(hidT_lo, 1)
                    if u == 5:
                        step(v.tensor_scalar(code[:], code[:], -float(P), None, ALU.add))
                        one_hot()
                    if kind == "down":
                        if u == 8:
                            dve.wait_ge(ysb_free, s + 1)
                        dve.wait_ge(y_part_ok, s * 4 + (u - 7))
                        v.tensor_tensor(y_sb[e * CAP:(e + 1) * CAP, half * BLK:(half + 1) * BLK],
                                        bank[0:CAP, 2 + 2 * half:4 + 2 * half, :].rearrange("p b n -> p (b n)"),
                                        y_part[:], ALU.add).then_inc(y_free, 1)

                for u in range(PAIR_UNITS):
                    for g in range(NG):
                        b = (u * NG + g) % NQ
                        dve.wait_ge(w_hi_ok, s * (PAIR_UNITS * NG) + (u * NG + g + 1))
                        v.tensor_tensor(w_lo[:, b, :], ring[:, u % RING, g * 1024:(g + 1) * 1024],
                                        w_hi[:, b, :].bitcast(F32), ALU.subtract).then_inc(w_lo_ok, 1)
                    if u:
                        after(u - 1)
                    if u >= 8:
                        f_i = 2 * (u - 8) + 1
                        gather_out(f_i, s * FILLS + (FILLS + f_i + 1))
                after(PAIR_UNITS - 1)

            PICK = 7

            def pick(done):
                step(v.tensor_scalar(in_pass[:], code[:], -float(PAIRS * P), None, ALU.is_ge))
                step(v.tensor_tensor(topw_now[:], topw[:], in_pass[:], ALU.mult))
                step(v.tensor_scalar(in_pass[:], code[:], 0.0, None, ALU.is_lt))
                step(v.tensor_tensor(topw_now[:], topw_now[:], in_pass[:], ALU.mult))
                step(v.tensor_scalar(in_pass[:], code[:], -float(PAIRS * P), -1.0, ALU.max, ALU.min))
                step(v.tensor_scalar(in_pass[:], in_pass[:], float(PAIRS * P), None, ALU.add))
                step(v.tensor_copy(rows[:], in_pass[:]))
                dve.sem_inc(done, 1)

            def between(r):
                chain.enter(r, PICK + 2 * TT + PAIRS * STEPS)
                pick(pick_ok)
                for i in range(2 * TT):
                    tt, j = i // 2, i % 2
                    dve.wait_ge(ysb_ld, r * (32 * TT) + 16 * (i + 1))
                    step(v.scalar_tensor_tensor(out=h[:, tt, :], in0=y_sb[:], scalar=topw_now[:, tt, j:j + 1],
                                                in1=h[:, tt, :], op0=ALU.mult, op1=ALU.add))
                    dve.sem_inc(ysb_used, 1)

            with dve.Fori(0, PAIRS) as s:
                pair(s, s)
            chain.leave(PAIRS)
            more_passes(dve, pair, between)
            chain.leave(PAIRS)
            chain.leave(PASSES - 1)
            chain = Chain(dve, last_c)
            pick(rows_ok)

            for tt in range(TT):
                for j in range(2):
                    dve.wait_ge(fetch[2 * tt + j], 16)
                    if j:
                        dve.wait_ge(fin_c, tt + 1)
                    ins = v.scalar_tensor_tensor(out=h[:, tt, :], in0=fetched[:, tt, j, :], scalar=topw_now[:, tt, j:j + 1],
                                                 in1=h[:, tt, :], op0=ALU.mult, op1=ALU.add)
                    ins.then_inc(res_ok if j else fin_c, 1)
            inverse_rms(ssq3, 24, var3, std3, inv3, D, TT)
            dve.wait_ge(gout_ld, 16)
            for tt in range(TT):
                dve.wait_ge(fin_s, tt + 1)
                v.tensor_tensor(h[:, tt, :], h[:, tt, :], gain_out[:], ALU.mult).then_inc(fin_ok, 1)


def constants():
    import math

    import numpy as np

    eye = np.eye(P, dtype=np.float32)
    pool = np.zeros((TOK, len(WINDOWS), TOK), np.float32)
    for g, w in enumerate(WINDOWS):
        for q in range(TOK):
            lo = max(0, q + 1 - w)
            pool[lo:q + 1, g, q] = np.float32(1.0) / np.float32(min(q + 1, w))
            pool[q, g, q] -= np.float32(1.0)
    n = np.arange(TOK)
    nf = np.maximum(n, 1).astype(np.float32)
    large = 16 + (np.log(nf / np.float32(16)) / np.float32(math.log(8.0)) * np.float32(16)).astype(np.int32)
    bucket = np.where(n < 16, n, np.minimum(large, 31))
    onehot = np.zeros((33, 2 * TOK), np.float32)
    for j in range(2 * TOK):
        onehot[bucket[TOK - 1 - j] if j < TOK else 32, j] = 1.0
    return {
        "c_eye": eye, "c_flip": np.ascontiguousarray(eye[::-1]), "c_pool": pool, "c_onehot": onehot,
        "c_tri": np.triu(np.ones((P, P), np.float32), 1), "c_ones": np.ones((P, P), np.float32),
        "c_iota": np.tile(np.arange(P, dtype=np.float32), (P, 1)),
    }


def kernel(**inputs):
    import numpy as np

    import concourse.bacc as bacc
    from concourse.bass_utils import run_bass_kernel_spmd as run

    a = {k: np.asarray(x) for k, x in inputs.items()}
    laid = {
        "x": a["x"][0],
        "table": a["rel_bias_table"],
        "gain_mix": a["norm_mix_gain"][0].reshape(KT, P).T,
        "w_in": a["w_in"][0],
        "w_gate": a["w_merge_gate"][0],
        "b_gate": a["b_merge_gate"][0],
        "pool_mix": a["pool_mix"][0],
        "pool_scale": a["pool_scale"][0].reshape(8, P).T,
        "w_up_pool": a["w_up_pool"][0],
        "lam": np.stack([a["lambda_q1"][0], a["lambda_k1"][0], a["lambda_q2"][0], a["lambda_k2"][0]]),
        "subln": a["subln_gain"][0].reshape(P, 1),
        "w_up_attn": a["w_up_attn"][0],
        "w_out": a["w_out"][0],
        "gain_ffn": a["norm_ffn_gain"][0],
        "w_rout": np.concatenate([a["w_router_group"][0],
                                  a["w_router_expert"][0].transpose(1, 0, 2).reshape(D, N_EXP)], axis=1),
        "b_rout": np.concatenate([a["b_router_group"][0], a["b_router_expert"][0].reshape(N_EXP)]),
        "w_e_gate": a["w_expert_gate"][0],
        "w_e_up": a["w_expert_up"][0],
        "w_e_down": a["w_expert_down"][0],
        "gain_out": a["final_norm_gain"],
    }
    laid.update(constants())
    nc = bacc.Bacc("TRN2", target_bir_lowering=False, num_devices=1)
    arrays, t = {}, {}
    for name, x in laid.items():
        x = np.ascontiguousarray(x)
        arrays["in_" + name] = x
        t[name] = nc.dram_tensor("in_" + name, x.shape, mybir.dt.from_np(x.dtype), kind="ExternalInput").ap()
    t["out"] = nc.dram_tensor("out", (TOK, D), F32, kind="ExternalOutput").ap()
    t["bias_dram"] = nc.dram_tensor("bias_dram", (HEADS, BANK), F32, kind="Internal").ap()
    t["y_rows"] = nc.dram_tensor("y_rows", (PAIRS * P, D), F32, kind="Internal").ap()
    build(nc, t)
    r = run(nc, [arrays], core_ids=[0])
    return r.results[0]["out"].reshape(1, TOK, D)
```

```python
from contextlib import ExitStack

import concourse.bass as bass
from concourse import mybir

F32 = mybir.dt.float32
F32R = mybir.dt.float32r
I32 = mybir.dt.int32
U32 = mybir.dt.uint32
ALU = mybir.AluOpType
ACT = mybir.ActivationFunctionType
AX = mybir.AxisListType.X

P = 128
TOK = 256
TT = TOK // P
D = 2048
KT = D // P
BLK = 1024
BANK = 512
RING = 4
UNIT = 4096
POOL_W = 1024
WINDOWS = (2, 4, 8, 16)
HEADS = 8
DH = 64
NEG = -1e30
EPS = 1e-6
LAMBDA_INIT = 0.2
N_GROUPS = 4
N_EXP = 32
F_EXP = 512
CAP = 64
PAIRS = N_EXP // 2
PASSES = TOK // CAP
PAIR_UNITS = 12
HALF = 2 * BLK
MIX_UNITS = 96
AHEAD = 4
NG = 3
NQ = 4
FILLS = KT // 2
ACT_FILLS, DVE_FILLS = (0, 2), (1, 3)
BIG = 1000.0


class Chain:

    def __init__(self, eng, sem):
        self.eng, self.sem, self.base, self.k, self.outer = eng, sem, 0, 0, []

    def step(self, ins):
        ins.then_inc(self.sem, 1)
        self.k += 1

    def settle(self):
        self.eng.wait_ge(self.sem, self.base + self.k)

    def enter(self, i, steps):
        self.outer.append((self.base, self.k, steps))
        self.base, self.k = self.base + self.k + i * steps, 0

    def leave(self, count):
        base, k, steps = self.outer.pop()
        assert self.k == steps, (self.k, steps)
        self.base, self.k = base, k + count * steps


def pair_units():
    return ([(k, e, h) for e in range(2) for k in ("gate", "up") for h in range(2)]
            + [("down", e, h) for e in range(2) for h in range(2)])


def build(nc, t):
    with ExitStack() as ctx:
        def sem(name):
            return ctx.enter_context(nc.semaphore(name))

        ctx.enter_context(nc.sbuf_tensor("fence", [P, 207 * 256], F32))
        first = 16512

        def at(name, kib, shape, dtype=F32):
            size = 4
            for n in shape[1:]:
                size *= n
            assert kib * 1024 + size <= 207 * 1024
            return nc.alloc_sbuf_tensor_at(name, shape, dtype, offset=first + int(kib * 1024))

        ring = at("ring", 0, [P, RING, UNIT])
        mring = at("mring", 0, [P, RING, HALF])
        m_hi = at("m_hi", 32, [P, AHEAD, BLK], F32R)
        m_lo = at("m_lo", 48, [P, AHEAD, BLK], F32R)
        b_gate = at("b_gate", 168, [P, BLK])
        xT_hi = at("xT_hi", 64, [P, KT, TOK], F32R)
        xT_lo = at("xT_lo", 144, [P, KT, TOK], F32R)
        x_in = at("x_in", 80, [P, TT, D])
        sq_junk = at("sq_junk", 144, [P, TT, D])
        bias_rows = at("bias_rows", 104, [HEADS, BANK])
        onehot = at("onehot", 172, [33, BANK])
        table = at("table", 174, [33, HEADS])
        lam_in = at("lam_in", 175, [P, 4, DH])
        lam_prod = at("lam_prod", 176, [P, 2, DH])
        flip = at("flip", 205.5, [P, P])
        proj = at("proj", 80, [P, TT, 4 * BLK])
        pool_at = at("pool_at", 112, [P, TT, 4, TOK])
        w_mix = at("w_mix", 120, [P, 8, 256])
        pooledT = at("pooledT", 128, [P, 8, TOK])
        hankel = at("hankel", 136, [P, HEADS, 256])
        gates = at("gates", 112, [P, TT, 4 * BLK])
        bias = at("bias", 160, [P, HEADS, 256])
        mixedT = at("mixedT", 172, [P, 8, TOK])
        oT = at("oT", 180, [P, HEADS, TOK])
        qk = at("qk", 188, [P, 2, TT, P])
        qkT = at("qkT", 190, [P, 2, TOK])
        probs = at("probs", 192, [P, 2, 384])
        amap = at("amap", 195, [P, 384])
        amapT = at("amapT", 196.5, [P, 384])
        o_n = at("o_n", 198, [P, TT, P])
        o_sq = at("o_sq", 199, [P, TT, P])
        mixT_hi = at("mixT_hi", 64, [P, 8, TOK], F32R)
        mixT_lo = at("mixT_lo", 72, [P, 8, TOK], F32R)
        oT_hi = at("oT_hi", 144, [P, 8, TOK], F32R)
        oT_lo = at("oT_lo", 152, [P, 8, TOK], F32R)
        merged = at("merged", 80, [P, TT, D])
        x_again = at("x_again", 96, [P, TT, D])
        mergT_hi = at("mergT_hi", 64, [P, KT, TOK], F32R)
        mergT_lo = at("mergT_lo", 112, [P, KT, TOK], F32R)
        h = at("h", 144, [P, TT, D])
        ident = at("ident", 200, [P, P])
        iota = at("iota", 200.5, [P, P])
        w_rout = at("w_rout", 201, [P, KT, 36])
        small = at("small", 203.5, [P, 224])
        tri = at("tri", 204.5, [P, P])
        ones = at("ones", 205, [P, P])
        gain_ffn = at("gain_ffn", 188, [P, D])
        hg = at("hg", 80, [P, TT, D])
        hT = at("hT", 166, [P, KT, TOK])
        sq2_junk = at("sq2_junk", 196, [P, BLK])
        rt = at("rt", 160, [P, TT, 8, 36])
        hn_hi = at("hn_hi", 112, [P, TT, KT, P], F32R)
        hn_lo = at("hn_lo", 128, [P, TT, KT, P], F32R)
        xg = at("xg", 64, [P, 2 * KT, 2, CAP], F32R)
        w_hi = at("w_hi", 80, [P, NQ, 1024], F32R)
        w_lo = at("w_lo", 96, [P, NQ, 1024], F32R)
        sel = at("sel", 163, [P, TT, P], F32R)
        sel12 = at("sel12", 164, [P, TT, 2, P])
        part = at("part", 166, [CAP, BANK])
        g_sb = at("g_sb", 168, [CAP, BANK])
        u_sb = at("u_sb", 170, [CAP, BANK])
        silu_g = at("silu_g", 172, [CAP, BANK])
        hid = at("hid", 174, [CAP, BANK])
        y_part = at("y_part", 176, [CAP, 2 * BANK])
        hidT = at("hidT", 180, [P, 2, 4, P], F32R)
        y_sb = at("y_sb", 188, [P, D])
        slot_row = at("slot_row", 196, [P, 1], U32)
        count = at("count", 196.25, [P, 1], I32)
        code = at("code", 196.5, [P, TT, 2])
        topw = at("topw", 197, [P, TT, 2])
        slot_f = at("slot_f", 197.5, [P, 1])
        fetched = at("fetched", 64, [P, TT, 2, D])
        gain_out = at("gain_out", 96, [P, D])
        sq3_junk = at("sq3_junk", 104, [P, D])

        gain_mix = small[:, 0:16]
        pool_scale = small[:, 16:24]
        subln = small[:, 24:25]
        stat = small[:, 32:64]
        b_rout = small[:, 64:100]
        lam_s = small[:, 100:108]
        sums = small[:, 108:112]
        nmax = small[:, 112:116]
        inv = small[:, 116:120]
        coef = small[:, 120:122]
        ssq_o = small[:, 122:124]
        var_o = small[:, 124:126]
        std_o = small[:, 126:128]
        inv_o = small[:, 128:130]
        nlam = small[:, 130:131]
        gain_o = small[:, 131:132]
        gain_fT = small[:, 132:148]
        ssq_h = small[:, 148:152]
        zero = stat[:, 17:18]
        idx12 = small[:, 152:156].rearrange("p (t j) -> p t j", t=TT)
        top12 = small[:, 156:160].rearrange("p (t j) -> p t j", t=TT)
        rank12 = small[:, 160:164].rearrange("p (t j) -> p t j", t=TT)
        row_of = small[:, 168:172].rearrange("p (t j) -> p t j", t=TT)
        over12 = small[:, 164:168].rearrange("p (t j) -> p t j", t=TT)

        bank = ctx.enter_context(nc.psum_tensor("bank", [P, 8, BANK], F32))

        landed = [sem(f"landed{i}") for i in range(RING)]
        unit_free = sem("unit_free")
        m_landed = [sem(f"m_landed{i}") for i in range(RING)]
        m_hi_ok, m_lo_ok, m_used = sem("m_hi_ok"), sem("m_lo_ok"), sem("m_used")
        x_ld = [sem(f"x_ld{i}") for i in range(TT)]
        bg_ld, xs_ok_d, pooledT_ok = sem("bg_ld"), sem("xs_ok_d"), sem("pooledT_ok")
        xT_hi_ok, xT_lo_ok, mix_hi_ok, mix_lo_ok, oT_hi_ok, oT_lo_ok, mT_hi_ok, mT_lo_ok = (
            sem(n) for n in ("xT_hi_ok", "xT_lo_ok", "mix_hi_ok", "mix_lo_ok", "oT_hi_ok", "oT_lo_ok", "mT_hi_ok",
                             "mT_lo_ok"))
        bg_used, flip_ld = sem("bg_used"), sem("flip_ld")
        id_ld, tab_ld, sm_ld, lam_ld = (sem(n) for n in ("id_ld", "tab_ld", "sm_ld", "lam_ld"))
        gmix_ld, zero_ok = sem("gmix_ld"), sem("zero_ok")
        pool_ld, hankel_ld, bias_st = (sem(n) for n in ("pool_ld", "hankel_ld", "bias_st"))
        x2_ld, gffn_ld, rout_ld, gout_ld = (sem(n) for n in ("x2_ld", "gffn_ld", "rout_ld", "gout_ld"))
        dve_c = sem("dve_chain")
        table_ok, bias_row_ps, bias_row_sb, flip_ps, bias_ok = (
            sem(n) for n in ("table_ok", "bias_row_ps", "bias_row_sb", "flip_ps", "bias_ok"))
        ssq1, var1, std1, inv1, xs_ok, xT_ps = (sem(n) for n in ("ssq1", "var1", "std1", "inv1", "xs_ok", "xT_ps"))
        emptied_a, emptied_d = sem("emptied_a"), sem("emptied_d")
        pooled_ps, low_free, mixed_ps, bank7_free = (
            sem(n) for n in ("pooled_ps", "low_free", "mixed_ps", "bank7_free"))
        lam_dot, lam_exp = sem("lam_dot"), sem("lam_exp")
        staged, qkT_ps, qkT_ok, s_ps, s_free, nmax_ok, p_ok = (
            sem(n) for n in ("staged", "qkT_ps", "qkT_ok", "s_ps", "s_free", "nmax_ok", "p_ok"))
        a_ok, aT_ps, aT_ok, o_ps, ssq_ok, var_ok, std_ok, on_ok, oT_ps = (
            sem(n) for n in ("a_ok", "aT_ps", "aT_ok", "o_ps", "ssq_ok", "var_ok", "std_ok", "on_ok", "oT_ps"))
        sig_ok, up_free, merged_ok, mT_ps, h_ok = (
            sem(n) for n in ("sig_ok", "up_free", "merged_ok", "mT_ps", "h_ok"))
        ssq2, var2, std2, inv2, hT_ps, hT_ok, hg_ok, hi_ok, lo_ok = (
            sem(n) for n in ("ssq2", "var2", "std2", "inv2", "hT_ps", "hT_ok", "hg_ok", "hi_ok", "lo_ok"))
        logit_ps, gdiff, gexp, mdiff, mexp, mask_ok, rank_ps, route_ok = (
            sem(n) for n in ("logit_ps", "gdiff", "gexp", "mdiff", "mexp", "mask_ok", "rank_ps", "route_ok"))
        sel_ok, gath_ps, gath_a, gath_d = (sem(n) for n in ("sel_ok", "gath_ps", "gath_a", "gath_d"))
        split_free, w_hi_ok, w_lo_ok = (sem(n) for n in ("split_free", "w_hi_ok", "w_lo_ok"))
        g_ps, g_part, g_sum, u_ps, u_part, hid_ok, hidT_ps, hidT_hi, hidT_lo = (
            sem(n) for n in ("g_ps", "g_part", "g_sum", "u_ps", "u_part", "hid_ok", "hidT_ps", "hidT_hi", "hidT_lo"))
        y_ps, y_part_ok, y_free, y_st, ysb_free = (
            sem(n) for n in ("y_ps", "y_part_ok", "y_free", "y_st", "ysb_free"))
        fetch = [[sem(f"fetch{i}_{j}") for j in range(2)] for i in range(TT)]
        held = sem("held")
        rowno_ld, slot_ps, slot_ok, all_st = (sem(n) for n in ("rowno_ld", "slot_ps", "slot_ok", "all_st"))
        fin_c, res_ok, ssq3, var3, std3, inv3, fin_s, fin_ok, out_st = (
            sem(n) for n in ("fin_c", "res_ok", "ssq3", "var3", "std3", "inv3", "fin_s", "fin_ok", "out_st"))

        units = pair_units()

        def unit_count(s, u):
            return (s * (PAIR_UNITS // RING) + (u // RING + 1)) * 16

        def more_passes(eng, body):
            eng.wait_ge(route_ok, 1)
            most = eng.value_load(count[0:1, 0:1], min_val=0, max_val=TOK)
            with eng.If(most > CAP):
                with eng.Fori(0, PASSES - 1) as r:
                    with eng.Fori(0, PAIRS) as q:
                        body(r * PAIRS + q + PAIRS, q)

        block = ctx.enter_context(nc.Block())

        @block.sync
        def _(sp):
            for tt in range(TT):
                sp.dma_start(x_in[:, tt, :], t["x"][tt * P:(tt + 1) * P, :]).then_inc(x_ld[tt], 16)

            def rows2(w, j, c0):
                return w[j * 2 * P:(j + 1) * 2 * P, bass.ds(c0, BLK)].rearrange("(t p) n -> p t n", p=P)

            def m_load(slot, src):
                sp.dma_start(mring[:, slot, :].rearrange("p (k n) -> p k n", n=BLK), src).then_inc(m_landed[slot], 16)

            for j in range(8):
                if j >= RING:
                    sp.wait_ge(m_lo_ok, 2 * (j - RING) + 2)
                m_load(j % RING, rows2(t["w_in"], j, 0))
            with sp.Fori(1, 4) as b:
                for j in range(8):
                    sp.wait_ge(m_lo_ok, b * 16 + (2 * (j - RING) + 2))
                    m_load(j % RING, rows2(t["w_in"], j, b * BLK))
            with sp.Fori(0, 4) as b:
                for j in range(8):
                    sp.wait_ge(m_lo_ok, b * 16 + (64 + 2 * (j - RING) + 2))
                    m_load(j % RING, rows2(t["w_gate"], j, b * BLK))
            m = 64
            for w, nblk, nj in (("w_up_pool", 2, 4), ("w_up_attn", 2, 4), ("w_out", 2, 8)):
                for b in range(nblk):
                    for j in range(nj):
                        sp.wait_ge(m_lo_ok, 2 * (m - RING) + 2)
                        m_load(m % RING, rows2(t[w], j, b * BLK))
                        m += 1

            def load(slot, src, cols):
                sp.dma_start(ring[:, slot, :].rearrange("p (k n) -> p k n", n=cols), src).then_inc(landed[slot], 16)

            sp.wait_ge(m_used, 2 * MIX_UNITS)
            sp.sem_inc(unit_free, RING)

            def pair(step, q):
                for u, (kind, e, half) in enumerate(units):
                    sp.wait_ge(unit_free, step * PAIR_UNITS + (u + 1))
                    expert = bass.ds(q * 2 + e, 1)
                    if kind == "down":
                        src = t["w_e_down"][expert, :, half * BLK:(half + 1) * BLK].rearrange(
                            "e (k p) n -> p (e k) n", p=P)
                        load(u % RING, src, BLK)
                    else:
                        src = t["w_e_" + kind][expert].rearrange("e (p k) n -> p (e k) n", p=P)
                        load(u % RING, src[:, half * 8:(half + 1) * 8, :], F_EXP)

            with sp.Fori(0, PAIRS) as s:
                pair(s, s)
            more_passes(sp, pair)
            sp.wait_ge(all_st, 1)
            y_tok = t["y_tok"].rearrange("(t p j) n -> t p (j n)", p=P, j=2)
            for tt in range(TT):
                for j in range(2):
                    sp.dma_start(fetched[:, tt, j, :], y_tok[tt][:, j * D:(j + 1) * D]).then_inc(fetch[tt][j], 16)
            sp.dma_start(gain_out[:], t["gain_out"].partition_broadcast(P)).then_inc(gout_ld, 16)
            for tt in range(TT):
                for half in range(2):
                    sp.wait_ge(fin_ok, 2 * tt + half + 1)
                    cols = slice(half * BLK, (half + 1) * BLK)
                    sp.dma_start(t["out"][tt * P:(tt + 1) * P, cols], h[:, tt, cols]).then_inc(out_st, 16)
            sp.wait_ge(out_st, 32 * TT)

        @block.gpsimd
        def _(pool):
            for tt in range(TT):
                pool.wait_ge(x_ld[tt], 16)
            pool.dma_start(pool_at[:], t["c_pool"].rearrange("(t p) g n -> p t g n", p=P)).then_inc(pool_ld, 16)
            pool.dma_start(w_mix[:], t["pool_mix"].rearrange("g (k p) n -> p (g k) n", p=P)).then_inc(pool_ld, 16)
            pool.dma_start(b_gate[:], t["b_gate"][0:BLK].partition_broadcast(P)).then_inc(bg_ld, 16)
            pool.wait_ge(bias_row_sb, 1)
            pool.dma_start(t["bias_dram"], bias_rows[:]).then_inc(bias_st, 16)
            pool.wait_ge(bias_st, 16)
            src = bass.AP(tensor=t["bias_dram"].tensor, offset=t["bias_dram"].offset, ap=[[1, P], [BANK, HEADS], [1, 256]])
            pool.dma_start(hankel[:], src).then_inc(hankel_ld, 16)
            pool.dma_start(w_rout[:], t["w_rout"].rearrange("(k p) n -> p k n", p=P)).then_inc(rout_ld, 16)
            pool.dma_start(b_rout, t["b_rout"].partition_broadcast(P)).then_inc(rout_ld, 16)
            pool.dma_start(tri[:], t["c_tri"]).then_inc(rout_ld, 16)
            pool.dma_start(ones[:], t["c_ones"]).then_inc(rout_ld, 16)
            pool.dma_start(iota[:], t["c_iota"]).then_inc(rout_ld, 16)
            pool.dma_start(row_of[:], t["c_rows"]).then_inc(rowno_ld, 16)
            for b in range(1, 4):
                pool.wait_ge(bg_used, b)
                pool.dma_start(b_gate[:], t["b_gate"][b * BLK:(b + 1) * BLK].partition_broadcast(P)).then_inc(bg_ld, 16)
            pool.wait_ge(bank7_free, HEADS + 1)
            pool.dma_start(gain_ffn[:], t["gain_ffn"].partition_broadcast(P)).then_inc(gffn_ld, 16)
            pool.dma_start(x_again[:], t["x"].rearrange("(t p) d -> p t d", p=P)).then_inc(x2_ld, 16)

            def pair(s, q):
                pool.wait_ge(y_free, s * 4 + 4)
                pool.sem_inc(held, 1)
                pool.indirect_dma_start(t["y_tok"], bass.IndirectOffsetOnAxis(ap=slot_row[:], axis=0), y_sb[:], None,
                                        bounds_check=2 * TOK - 1, oob_is_err=False).then_inc(y_st, 16)
                pool.wait_ge(y_st, s * 16 + 16)
                pool.sem_inc(ysb_free, 1)

            with pool.Fori(0, PAIRS) as s:
                pair(s, s)
            more_passes(pool, pair)
            pool.sem_inc(all_st, 1)

        @block.tensor
        def _(pe):
            mm = nc.tensor.matmul

            def transposes(src, f, out_bank, done):
                for i in range(2):
                    for tt in range(TT):
                        c = (2 * f + i) * P
                        last = nc.tensor.transpose(bank[:, out_bank, i * TOK + tt * P:i * TOK + (tt + 1) * P],
                                                   src[:, tt, c:c + P], ident[:])
                last.then_inc(done, 1)

            pe.wait_ge(id_ld, 16)
            pe.wait_ge(xs_ok, 1)
            pe.wait_ge(xs_ok_d, 1)
            for f in range(7):
                transposes(x_in, f, f, xT_ps)
            pe.wait_ge(tab_ld, 32)
            pe.wait_ge(table_ok, 1)
            mm(bank[0:HEADS, 7, :], table[:], onehot[:], start=True, stop=True).then_inc(bias_row_ps, 1)
            pe.wait_ge(bias_row_sb, 1)
            transposes(x_in, 7, 7, xT_ps)

            def tile(base, i, hi, lo, k, head, tail, bank0, wait_bank=None):
                b = i % AHEAD
                pe.wait_ge(m_lo_ok, base + (i + 1))
                for c in range(2):
                    cols = slice(c * BANK, (c + 1) * BANK)
                    for tt in range(TT):
                        if wait_bank:
                            wait_bank(2 * c + tt)
                        toks, out = slice(tt * P, (tt + 1) * P), bank[:, bank0 + 2 * c + tt, :]
                        mm(out, hi[:, k, toks], m_hi[:, b, cols], start=head, stop=False)
                        mm(out, lo[:, k, toks], m_hi[:, b, cols], start=False, stop=False)
                        last = mm(out, hi[:, k, toks], m_lo[:, b, cols], start=False, stop=tail)
                last.then_inc(m_used, 1)

            pe.wait_ge(xT_lo_ok, 4)
            with pe.Fori(0, 2) as b:
                for half in range(2):
                    pe.wait_ge(emptied_a, b * 4 + (2 * half + 2))
                    pe.wait_ge(emptied_d, b * 4 + (2 * half + 2))
                    for k in range(KT):
                        if k >= 8 and k % 2 == 0:
                            pe.wait_ge(xT_lo_ok, k // 2 + 1)
                        tile(b * 32, 16 * half + k, xT_hi, xT_lo, k, k == 0, k == KT - 1, 4 * half)

            pe.wait_ge(hankel_ld, 16)
            pe.wait_ge(flip_ld, 16)
            pe.wait_ge(emptied_a, 10)
            pe.wait_ge(emptied_d, 10)
            for i in range(4):
                mm(bank[:, i, :], flip[:], hankel[:, 2 * i:2 * i + 2, :], start=True, stop=True).then_inc(flip_ps, 1)
            pe.wait_ge(pool_ld, 32)
            pe.wait_ge(emptied_a, 12)
            pe.wait_ge(emptied_d, 12)
            for c in range(8):
                g = c // 2
                for tt in range(TT):
                    last = mm(bank[:, 4 + c // 2, (c % 2) * TOK + tt * P:(c % 2 + 1) * TOK],
                              proj[:, tt, c * P:(c + 1) * P], pool_at[:, tt, g, tt * P:TOK],
                              start=tt == 0, stop=tt == TT - 1)
                if c % 2:
                    last.then_inc(pooled_ps, 1)
            pe.wait_ge(bias_ok, 4)
            pe.wait_ge(pooledT_ok, 4)
            for g in range(4):
                for m in range(2):
                    for k in range(2):
                        last = mm(bank[:, g, m * TOK:(m + 1) * TOK], w_mix[:, 2 * g + k, m * P:(m + 1) * P],
                                  pooledT[:, 2 * g + k, :], start=k == 0, stop=k == 1)
                last.then_inc(mixed_ps, 1)

            def head_transpose(n):
                pe.wait_ge(staged, n)
                for a in range(2):
                    for tt in range(TT):
                        last = nc.tensor.transpose(bank[:, 4, a * TOK + tt * P:a * TOK + (tt + 1) * P],
                                                   qk[:, a, tt, :], ident[:])
                last.then_inc(qkT_ps, 1)

            def head_scores(n):
                pe.wait_ge(qkT_ok, n)
                for c in range(2):
                    lanes = slice(DH * c, DH * c + DH)
                    mm(bank[:, 5 + c, 0:P], qkT[lanes, 0, 0:P], qkT[lanes, 1, 0:P], start=True, stop=True)
                    last = mm(bank[:, 5 + c, P:P + TOK], qkT[lanes, 0, P:TOK], qkT[lanes, 1, :], start=True, stop=True)
                last.then_inc(s_ps, 1)

            def head_map_transpose(n):
                pe.wait_ge(a_ok, n)
                pe.wait_ge(bank7_free, n)
                for i in range(3):
                    last = nc.tensor.transpose(bank[:, 7, i * P:(i + 1) * P], amap[:, i * P:(i + 1) * P], ident[:])
                last.then_inc(aT_ps, 1)

            def head_values(n, head):
                pe.wait_ge(aT_ok, n)
                v = [proj[:, tt, bass.ds(head * P + 3 * BLK, P)] for tt in range(TT)]
                mm(bank[:, 4, 0:P], amapT[:, 0:P], v[0], start=True, stop=True)
                mm(bank[:, 4, P:2 * P], amapT[:, P:2 * P], v[0], start=True, stop=False)
                mm(bank[:, 4, P:2 * P], amapT[:, 2 * P:3 * P], v[1], start=False, stop=True).then_inc(o_ps, 1)

            def head_out_transpose(n):
                pe.wait_ge(on_ok, n)
                for tt in range(TT):
                    last = nc.tensor.transpose(bank[:, 7, tt * P:(tt + 1) * P], o_n[:, tt, :], ident[:])
                last.then_inc(oT_ps, 1)

            with pe.Fori(0, 4) as b:
                for k in range(KT):
                    hh, point = divmod(k, 8)
                    n = b * 2 + (hh + 1)
                    if k == 8:
                        head_out_transpose(b * 2 + 1)
                    if point == 1:
                        head_transpose(n)
                    if point == 2:
                        head_scores(n)
                    if point == 5:
                        head_map_transpose(n)
                    if point == 6:
                        head_values(n, b * 2 + hh)
                    tile(b * 16 + 64, k, xT_hi, xT_lo, k, k == 0, k == KT - 1, 0,
                         (lambda i: pe.wait_ge(low_free, b * 4 + (i + 1))) if k == 0 else None)
                head_out_transpose(b * 2 + 2)

            base = 8 * KT
            pe.wait_ge(low_free, 20)
            pe.wait_ge(mix_lo_ok, 1)
            for b in range(4):
                if b == 1:
                    pe.wait_ge(bank7_free, HEADS + 1)
                if b == 2:
                    pe.wait_ge(oT_lo_ok, 1)
                hi, lo = (mixT_hi, mixT_lo) if b < 2 else (oT_hi, oT_lo)
                for k in range(8):
                    if b == 0 and k == 4:
                        pe.wait_ge(mix_lo_ok, 2)
                    if b == 3 and k == 4:
                        pe.wait_ge(merged_ok, 1)
                        for f in range(4):
                            transposes(merged, f, f, mT_ps)
                    tile(base, 8 * b + k, hi, lo, k, k == 0, k == 7, 4 * (b % 2),
                         (lambda i: pe.wait_ge(up_free, 4 * (b - 2) + i + 1)) if b >= 2 and k == 0 else None)
            pe.wait_ge(mT_lo_ok, 4)
            for b in range(2):
                for k in range(KT):
                    if b == 0 and k == 4:
                        pe.wait_ge(merged_ok, 2)
                        for f in range(4, 8):
                            transposes(merged, f, f, mT_ps)
                    if b == 0 and k == 8:
                        pe.wait_ge(mT_lo_ok, 8)
                    if b == 1 and k == 8:
                        pe.wait_ge(h_ok, 4)
                        for f in range(4):
                            transposes(h, f, f, hT_ps)
                    tile(base, 32 + 16 * b + k, mergT_hi, mergT_lo, k, k == 0, k == KT - 1, 4 * b)
            pe.wait_ge(hT_ok, 4)
            pe.wait_ge(rout_ld, 80)
            for k in range(KT):
                if k == 5:
                    pe.wait_ge(h_ok, 8)
                    for f in range(4, 8):
                        transposes(h, f, f, hT_ps)
                if k >= 8 and k % 2 == 0:
                    pe.wait_ge(hT_ok, k // 2 + 1)
                for tt in range(TT):
                    last = mm(bank[:, 2 + tt, 0:36], hT[:, k, tt * P:(tt + 1) * P], w_rout[:, k, :],
                              start=k == 0, stop=k == KT - 1)
            last.then_inc(logit_ps, 1)
            pe.wait_ge(mask_ok, 1)
            mask = rt[:, :, 6, 0:32]
            mm(bank[:, 5, 0:32], tri[:], mask[:, 0, :], start=True, stop=True)
            mm(bank[:, 5, 32:64], ones[:], mask[:, 0, :], start=True, stop=False)
            mm(bank[:, 5, 32:64], tri[:], mask[:, 1, :], start=False, stop=True).then_inc(rank_ps, 1)
            mm(bank[:, 4, 0:32], ones[:], mask[:, 0, :], start=True, stop=False)
            mm(bank[:, 4, 0:32], ones[:], mask[:, 1, :], start=False, stop=True).then_inc(rank_ps, 1)

            def gather_part(f, part_i, out_bank):
                for i in range(2):
                    c = part_i * 256 + i * P
                    for tt in range(TT):
                        last = mm(bank[:, out_bank, c:c + P], (hn_hi, hn_lo)[part_i][:, tt, 2 * f + i, :],
                                  sel[:, tt, :], start=tt == 0, stop=tt == TT - 1)
                return last

            def gather_fill(f, out_bank=7):
                gather_part(f, 0, out_bank)
                gather_part(f, 1, out_bank).then_inc(gath_ps, 1)

            pe.wait_ge(rowno_ld, 16)
            pe.wait_ge(hi_ok, TT)
            pe.wait_ge(sel_ok, 1)
            for f in ACT_FILLS + DVE_FILLS:
                gather_part(f, 0, f)
            pe.wait_ge(lo_ok, TT)
            for f in ACT_FILLS:
                gather_part(f, 1, f).then_inc(gath_ps, 1)
            pe.wait_ge(lo_ok, 2 * TT)
            pe.sem_inc(split_free, NQ)
            for f in DVE_FILLS:
                gather_part(f, 1, f).then_inc(gath_ps, 1)

            first = 2 * NG

            def pair(s, _):
                for u, (kind, e, half) in enumerate(units):
                    slot = u % RING
                    if u == 0:
                        pe.wait_ge(gath_a, s * 4 + 2)
                        pe.wait_ge(gath_d, s * 4 + 2)
                    if u == 1:
                        for f in range(FILLS // 2, FILLS):
                            if f == 6:
                                pe.wait_ge(gath_a, s * 4 + 3)
                            if f == 7:
                                pe.wait_ge(gath_d, s * 4 + 3)
                            gather_fill(f, 7 - f % 2)
                        pe.wait_ge(gath_a, s * 4 + 4)
                        pe.wait_ge(gath_d, s * 4 + 4)
                    if u == 8:
                        pe.wait_ge(hidT_lo, s * 2 + 1)
                        pe.wait_ge(sel_ok, s + 2)
                    if u == 10:
                        pe.wait_ge(hidT_lo, s * 2 + 2)
                    if u >= 10:
                        pe.wait_ge(y_free, s * 4 + (u - 9))
                    if u >= 8:
                        f = u - 8
                        if f:
                            pe.wait_ge(gath_a if f % 2 else gath_d, s * 4 + (4 + (f + 1) // 2))
                        gather_fill(f)
                    pe.wait_ge(landed[slot], unit_count(s, u))

                    def tile(i, moving_hi, moving_lo):
                        if kind == "down":
                            k, c = i // 2, i % 2
                            stat_op, out = hidT[:, e, k, :], bank[:, 2 + 2 * half + c, :]
                            head, tail = i in (first, 1), i in (first - 2, 7)
                        else:
                            k = 8 * half + i
                            stat_op, out = xg[:, 2 * k + e, :, :], bank[:, 0 if kind == "gate" else 1, :]
                            head, tail = half == 0 and i == first, half == 1 and i == 7
                        if moving_hi is None:
                            return mm(out, stat_op.bitcast(F32), ring[:, slot, i * BANK:(i + 1) * BANK],
                                      start=head, stop=tail)
                        mm(out, stat_op, moving_hi, start=head, stop=False)
                        return mm(out, stat_op, moving_lo, start=False, stop=tail)

                    tile(first, None, None)
                    for g in range(NG):
                        n = s * (PAIR_UNITS * NG) + (u * NG + g + 1)
                        b = (u * NG + g) % NQ
                        pe.wait_ge(w_lo_ok, n)
                        for i in range(2):
                            last = tile(2 * g + i, w_hi[:, b, i * BANK:(i + 1) * BANK], w_lo[:, b, i * BANK:(i + 1) * BANK])
                        last.then_inc(split_free, 1)
                    for i in range(first + 1, 8):
                        if i == 7 and u in (4, 8):
                            pe.wait_ge(hid_ok, s * 2 + (u // 4))
                        last = tile(i, None, None)
                    last.then_inc(unit_free, 1)
                    if u == 2:
                        for tt in range(TT):
                            for j in range(2):
                                last = mm(bank[:, 6, 0:1], sel12[:, tt, j, :], row_of[:, tt, j:j + 1],
                                          start=tt + j == 0, stop=tt + j == TT)
                        last.then_inc(slot_ps, 1)
                    if u in (4, 8):
                        for k in range(4):
                            last = nc.tensor.transpose(bank[:, 6, k * CAP:(k + 1) * CAP], hid[:, k * P:(k + 1) * P],
                                                       ident[0:CAP, 0:CAP])
                        last.then_inc(hidT_ps, 1)

            with pe.Fori(0, PAIRS) as s:
                pair(s, s)
            more_passes(pe, pair)

        @block.scalar
        def _(act):
            f = nc.scalar.activation
            act.dma_start(ident[:], t["c_eye"]).then_inc(id_ld, 16)
            act.dma_start(gain_mix, t["gain_mix"]).then_inc(gmix_ld, 16)
            act.dma_start(table[0:32, :], t["table"]).then_inc(tab_ld, 16)
            act.dma_start(onehot[:], t["c_onehot"]).then_inc(tab_ld, 16)
            warm = stat[:, 16:17]
            act.wait_ge(zero_ok, 1)
            f(warm, zero, ACT.Sqrt)
            act.sem_inc(emptied_a, 4)
            act.sem_inc(bank7_free, 1)

            for tt in range(TT):
                act.wait_ge(x_ld[tt], 16)
                f(sq_junk[:, tt, :], x_in[:, tt, :], ACT.Square, accum_out=stat[:, tt:tt + 1]).then_inc(ssq1, 1)
            act.wait_ge(var1, 1)
            f(stat[:, 4:6], stat[:, 2:4], ACT.Sqrt).then_inc(std1, 1)
            act.wait_ge(inv1, 1)
            f(x_in[:, 0, :], x_in[:, 0, :], ACT.Copy, scale=stat[:, 6:7]).then_inc(xs_ok, 1)
            act.dma_start(pool_scale, t["pool_scale"]).then_inc(sm_ld, 16)
            act.dma_start(subln, t["subln"]).then_inc(sm_ld, 16)
            act.dma_start(gain_fT, t["gain_fT"]).then_inc(sm_ld, 16)
            act.dma_start(lam_in[:], t["lam"].partition_broadcast(P)).then_inc(lam_ld, 16)
            act.dma_start(flip[:], t["c_flip"]).then_inc(flip_ld, 16)
            act.wait_ge(gmix_ld, 16)

            def split(base, i, first=False):
                if i % 2 == 0:
                    act.wait_ge(m_landed[(i // 2) % RING], base * 2 + 16 * (i // 8 + 1))
                if not first:
                    act.wait_ge(m_used, base + (i - AHEAD + 1))
                f(m_hi[:, i % AHEAD, :], mring[:, (i // 2) % RING, (i % 2) * BLK:(i % 2 + 1) * BLK],
                  ACT.Copy).then_inc(m_hi_ok, 1)

            for b in range(8):
                act.wait_ge(xT_ps, b + 1)
                for i in range(2):
                    k = 2 * b + i
                    last = f(xT_hi[:, k, :], bank[:, b, i * TOK:(i + 1) * TOK], ACT.Copy, scale=gain_mix[:, k:k + 1])
                last.then_inc(xT_hi_ok, 1)
                if b == 3:
                    split(0, 0, True)
            for i in range(1, AHEAD):
                split(0, i, True)
            act.wait_ge(sm_ld, 48)
            act.wait_ge(lam_dot, 1)
            f(lam_s[:, 2:4], lam_s[:, 0:2], ACT.Exp).then_inc(lam_exp, 1)

            with act.Fori(0, 2) as b:
                for i in range(AHEAD, 2 * KT + AHEAD):
                    split(b * 32, i)
                    if i % KT == AHEAD - 1:
                        half = i // KT - 1
                        act.wait_ge(m_used, b * 32 + KT * (half + 1))
                        for tt in range(TT):
                            f(proj[:, tt, bass.ds(b * (2 * BLK) + half * BLK, BANK)], bank[:, 4 * half + tt, :],
                              ACT.Copy).then_inc(emptied_a, 1)
            for b in range(4):
                act.wait_ge(pooled_ps, b + 1)
                f(pooledT[:, 2 * b:2 * b + 2, :].rearrange("p k n -> p (k n)"), bank[:, 4 + b, :],
                  ACT.Copy).then_inc(pooledT_ok, 1)
            act.wait_ge(emptied_d, 12)
            act.wait_ge(emptied_a, 12)

            def stage(n, head):
                for a, scale in ((0, float(DH) ** -0.5), (1, 1.0)):
                    last = f(qk[:, a, :, :], proj[:, :, bass.ds(head * P + (1 + a) * BLK, P)], ACT.Copy, scale=scale)
                last.then_inc(staged, 1)

            with act.Fori(0, 4) as b:
                stage(b * 2 + 1, b * 2)
                for i in range(AHEAD, KT + AHEAD):
                    hh, point = divmod(i - AHEAD, 8)
                    n, head = b * 2 + (hh + 1), b * 2 + hh
                    if point != 2:
                        split(b * 16 + 64, i)
                    if point == 0:
                        act.wait_ge(qkT_ps, n)
                        f(qkT[:].rearrange("p a n -> p (a n)"), bank[:, 4, :], ACT.Copy).then_inc(qkT_ok, 1)
                        f(warm, zero, ACT.Exp)
                    if point == 2:
                        act.wait_ge(nmax_ok, n)
                        for qt, (lo, hi) in enumerate(((0, P), (P, 3 * P))):
                            for c in range(2):
                                j = 2 * qt + c
                                last = f(probs[:, c, lo:hi], probs[:, c, lo:hi], ACT.Exp, bias=nmax[:, j:j + 1],
                                         accum_out=sums[:, j:j + 1])
                        last.then_inc(p_ok, 1)
                        split(b * 16 + 64, i)
                    if point == 4:
                        act.wait_ge(aT_ps, n)
                        f(amapT[:], bank[:, 7, 0:3 * P], ACT.Copy).then_inc(aT_ok, 1)
                        f(warm, zero, ACT.Sqrt)
                    if point == 5:
                        act.wait_ge(o_ps, n)
                        for tt in range(TT):
                            last = f(o_sq[:, tt, :], bank[:, 4, tt * P:(tt + 1) * P], ACT.Square,
                                     accum_out=ssq_o[:, tt:tt + 1])
                        last.then_inc(ssq_ok, 1)
                        act.wait_ge(var_ok, n)
                        f(std_o, var_o, ACT.Sqrt).then_inc(std_ok, 1)
                    if point == 6 and hh == 0:
                        stage(b * 2 + 2, b * 2 + 1)
                    if point == 7:
                        act.wait_ge(oT_ps, n)
                        f(oT[:, bass.ds(head, 1), :].rearrange("p a n -> p (a n)"), bank[:, 7, 0:TOK], ACT.Copy,
                          scale=gain_o).then_inc(bank7_free, 1)

            act.wait_ge(m_used, 8 * KT)
            for i in range(2):
                f(mixT_hi[:, 4 * i:4 * i + 4, :], mixedT[:, 4 * i:4 * i + 4, :], ACT.Copy).then_inc(mix_hi_ok, 1)

            def high_transposed(f0):
                for g in range(f0, f0 + 4):
                    act.wait_ge(mT_ps, g + 1)
                    f(mergT_hi[:, 2 * g:2 * g + 2, :].rearrange("p k n -> p (k n)"), bank[:, g, :],
                      ACT.Copy).then_inc(mT_hi_ok, 1)

            def h_transposed(f0):
                for g in range(f0, f0 + 4):
                    act.wait_ge(hT_ps, g + 1)
                    for i in range(2):
                        k = 2 * g + i
                        last = f(hT[:, k, :], bank[:, g, i * TOK:(i + 1) * TOK], ACT.Copy, scale=gain_fT[:, k:k + 1])
                    last.then_inc(hT_ok, 1)

            def squares(b):
                for tt in range(TT):
                    j = 2 * b + tt
                    act.wait_ge(h_ok, 4 * b + 2 * tt + 2)
                    if j:
                        act.wait_ge(ssq2, j)
                    f(sq2_junk[:], h[:, tt, b * BLK:(b + 1) * BLK], ACT.Square,
                      accum_out=ssq_h[:, j:j + 1]).then_inc(ssq2, 1)

            for i in range(AHEAD, 64):
                split(8 * KT, i)
                if i < AHEAD + 4:
                    b = i - AHEAD
                    act.wait_ge(low_free, b * 4 + 8)
                    cols = slice(b * BLK, (b + 1) * BLK)
                    f(gates[:, :, cols], gates[:, :, cols], ACT.Sigmoid).then_inc(sig_ok, 1)
                if i == 9:
                    act.wait_ge(bank7_free, HEADS + 1)
                    f(oT_hi[:], oT[:], ACT.Copy).then_inc(oT_hi_ok, 1)
                if i == 28 + AHEAD - 1:
                    high_transposed(0)
                if i == 36 + AHEAD - 1:
                    high_transposed(4)
                if i == 48 + AHEAD:
                    squares(0)
                if i == 56 + AHEAD - 1:
                    h_transposed(0)
            squares(1)
            h_transposed(4)
            act.wait_ge(var2, 1)
            f(stat[:, 12:14], stat[:, 10:12], ACT.Sqrt).then_inc(std2, 1)
            act.wait_ge(inv2, 1)
            act.wait_ge(hg_ok, 2 * TT)
            for tt in range(TT):
                f(hn_hi[:, tt, :, :], hg[:, tt, :].rearrange("p (q k) -> p k q", k=KT), ACT.Copy,
                  scale=stat[:, 14 + tt:15 + tt]).then_inc(hi_ok, 1)
            act.wait_ge(gdiff, 1)
            f(rt[:, :, 1, 0:4], rt[:, :, 1, 0:4], ACT.Exp).then_inc(gexp, 1)
            act.wait_ge(mdiff, 1)
            f(stat[:, 20:22], stat[:, 18:20], ACT.Exp).then_inc(mexp, 1)
            f(stat[:, 16:18], stat[:, 18:20], ACT.Silu)

            def gather_out(f_i, n, b=7):
                act.wait_ge(gath_ps, n)
                src = bank[:, b, :].rearrange("p (a c s) -> p a c s", a=2, s=CAP)
                f(xg[:, 4 * f_i:4 * f_i + 4, :, :].rearrange("p c a s -> p a c s"), src, ACT.Copy).then_inc(gath_a, 1)

            for n, f_i in enumerate(ACT_FILLS):
                gather_out(f_i, n + 1, f_i)

            def pair(s, q):
                def after(u):
                    kind, e, half = units[u]
                    n = s * 2 + (e + 1)
                    done = s * PAIR_UNITS + (RING + u + 1)
                    if kind == "gate" and half == 1:
                        act.wait_ge(unit_free, done)
                        f(part[:], bank[CAP:P, 0, :], ACT.Copy).then_inc(g_part, 1)
                    if kind == "up" and half == 1:
                        act.wait_ge(g_sum, n)
                        f(silu_g[:], g_sb[:], ACT.Silu)
                        act.wait_ge(unit_free, done)
                        f(part[:], bank[CAP:P, 1, :], ACT.Copy).then_inc(u_part, 1)
                    if u in (4, 8):
                        act.wait_ge(hidT_ps, s * 2 + (u // 4))
                        f(hidT[:, u // 4 - 1, :, 0:CAP], bank[:, 6, 0:4 * CAP].rearrange("p (k s) -> p k s", s=CAP),
                          ACT.Copy).then_inc(hidT_hi, 1)
                    if kind == "down":
                        act.wait_ge(unit_free, done)
                        if u > 8:
                            act.wait_ge(y_free, s * 4 + (u - 8))
                        f(y_part[:], bank[CAP:P, 2 + 2 * half:4 + 2 * half, :].rearrange("p b n -> p (b n)"),
                          ACT.Copy).then_inc(y_part_ok, 1)

                for u in range(PAIR_UNITS):
                    act.wait_ge(landed[u % RING], unit_count(s, u))
                    for g in range(NG):
                        b = (u * NG + g) % NQ
                        act.wait_ge(split_free, s * (PAIR_UNITS * NG) + (u * NG + g + 1))
                        f(w_hi[:, b, :], ring[:, u % RING, g * 1024:(g + 1) * 1024], ACT.Copy).then_inc(w_hi_ok, 1)
                        if u == 1 and g == 0:
                            for f_i in range(FILLS // 2, FILLS, 2):
                                gather_out(f_i, s * FILLS + (f_i + 1), 7)
                    if u in (8, 10):
                        gather_out(u - 8, s * FILLS + (FILLS + (u - 8) + 1))
                    if u:
                        after(u - 1)
                after(PAIR_UNITS - 1)

            with act.Fori(0, PAIRS) as s:
                pair(s, s)
            more_passes(act, pair)

            for tt in range(TT):
                act.wait_ge(res_ok, tt + 1)
                if tt:
                    act.wait_ge(ssq3, tt)
                f(sq3_junk[:], h[:, tt, :], ACT.Square, accum_out=stat[:, 24 + tt:25 + tt]).then_inc(ssq3, 1)
                act.wait_ge(var3, tt + 1)
                f(stat[:, 28 + tt:29 + tt], stat[:, 26 + tt:27 + tt], ACT.Sqrt).then_inc(std3, 1)

        @block.vector
        def _(dve):
            v = nc.vector
            chain = Chain(dve, dve_c)

            def step(ins):
                chain.step(ins)
                chain.settle()

            v.memset(table[32:33, :], NEG).then_inc(table_ok, 1)
            dve.sem_inc(emptied_d, 4)
            v.memset(zero, 0.0).then_inc(zero_ok, 1)

            def inverse_rms(ssq_sem, c, var_sem, std_sem, inv_sem, width, n):
                dve.wait_ge(ssq_sem, n)
                v.tensor_scalar(stat[:, c + 2:c + 4], stat[:, c:c + 2], 1.0 / width, EPS, ALU.mult, ALU.add).then_inc(var_sem, 1)
                dve.wait_ge(std_sem, 1)
                v.reciprocal(stat[:, c + 6:c + 8], stat[:, c + 4:c + 6]).then_inc(inv_sem, 1)

            inverse_rms(ssq1, 0, var1, std1, inv1, D, TT)
            dve.wait_ge(x_ld[1], 16)
            dve.wait_ge(inv1, 1)
            v.tensor_scalar(x_in[:, 1, :], x_in[:, 1, :], stat[:, 7:8], None, ALU.mult).then_inc(xs_ok_d, 1)
            dve.wait_ge(gmix_ld, 16)

            def split(base, i):
                dve.wait_ge(m_hi_ok, base + (i + 1))
                v.tensor_tensor(m_lo[:, i % AHEAD, :], mring[:, (i // 2) % RING, (i % 2) * BLK:(i % 2 + 1) * BLK],
                                m_hi[:, i % AHEAD, :].bitcast(F32), ALU.subtract).then_inc(m_lo_ok, 1)

            for b in range(8):
                dve.wait_ge(xT_hi_ok, b + 1)
                for i in range(2):
                    k = 2 * b + i
                    last = v.scalar_tensor_tensor(out=xT_lo[:, k, :], in0=bank[:, b, i * TOK:(i + 1) * TOK],
                                                  scalar=gain_mix[:, k:k + 1], in1=xT_hi[:, k, :].bitcast(F32),
                                                  op0=ALU.mult, op1=ALU.subtract)
                last.then_inc(xT_lo_ok, 1)
                if b == 3:
                    split(0, 0)
                    dve.wait_ge(bias_row_ps, 1)
                    v.tensor_copy(bias_rows[:], bank[0:HEADS, 7, :]).then_inc(bias_row_sb, 1)
            for i in range(1, AHEAD):
                split(0, i)
            dve.wait_ge(sm_ld, 48)
            step(v.tensor_scalar(gain_o, subln, 1.0 - LAMBDA_INIT, None, ALU.mult))
            dve.wait_ge(lam_ld, 16)
            lam_v = lam_in[:].rearrange("p (a b) n -> p a b n", b=2)
            step(v.tensor_tensor(lam_prod[:], lam_v[:, :, 0, :], lam_v[:, :, 1, :], ALU.mult))
            v.tensor_reduce(lam_s[:, 0:2], lam_prod[:], AX, ALU.add).then_inc(lam_dot, 1)
            dve.wait_ge(lam_exp, 1)
            step(v.tensor_tensor(lam_s[:, 4:5], lam_s[:, 3:4], lam_s[:, 2:3], ALU.subtract))
            step(v.tensor_scalar(nlam, lam_s[:, 4:5], -LAMBDA_INIT, None, ALU.add))

            dve.wait_ge(bias_st, 16)
            with dve.Fori(0, 2) as b:
                for i in range(AHEAD, 2 * KT + AHEAD):
                    split(b * 32, i)
                    if i % KT == AHEAD - 1:
                        half = i // KT - 1
                        dve.wait_ge(m_used, b * 32 + KT * (half + 1))
                        for tt in range(TT):
                            v.tensor_copy(proj[:, tt, bass.ds(b * (2 * BLK) + (half * BLK + BANK), BANK)],
                                          bank[:, 4 * half + 2 + tt, :]).then_inc(emptied_d, 1)
            for i in range(4):
                dve.wait_ge(flip_ps, i + 1)
                v.tensor_copy(bias[:, 2 * i:2 * i + 2, :], bank[:, i, :].rearrange("p (a n) -> p a n", a=2)).then_inc(bias_ok, 1)
            for g in range(4):
                dve.wait_ge(mixed_ps, g + 1)
                for m in range(2):
                    c = 2 * g + m
                    last = v.tensor_scalar(mixedT[:, c, :], bank[:, g, m * TOK:(m + 1) * TOK],
                                           pool_scale[:, c:c + 1], None, ALU.mult)
                last.then_inc(low_free, 1)
            dve.wait_ge(bias_ok, 4)

            with dve.Fori(0, 4) as b:
                chain.enter(b, 10)
                for i in range(AHEAD, KT + AHEAD):
                    hh, point = divmod(i - AHEAD, 8)
                    n, head = b * 2 + (hh + 1), b * 2 + hh
                    if point not in (1, 2):
                        split(b * 16 + 64, i)
                    if point == 1:
                        dve.wait_ge(s_ps, n)
                        hbias = bias[:, bass.ds(head, 1), :]
                        v.tensor_tensor(probs[:, :, 0:P], bank[:, 5:7, 0:P],
                                        hbias[:, :, P:2 * P].to_broadcast([P, 2, P]), ALU.add)
                        v.tensor_tensor(probs[:, :, P:3 * P], bank[:, 5:7, P:3 * P],
                                        hbias.to_broadcast([P, 2, 2 * P]), ALU.add).then_inc(s_free, 1)
                        dve.wait_ge(s_free, n)
                        v.tensor_reduce(nmax[:, 0:2], probs[:, :, 0:P], AX, ALU.max, negate=True)
                        v.tensor_reduce(nmax[:, 2:4], probs[:, :, P:3 * P], AX, ALU.max, negate=True).then_inc(nmax_ok, 1)
                        split(b * 16 + 64, i)
                    if point == 2:
                        dve.wait_ge(p_ok, n)
                        step(v.reciprocal(inv, sums))
                        step(v.tensor_scalar(coef, inv.rearrange("p (q c) -> p q c", c=2)[:, :, 1], nlam, None, ALU.mult))
                        chain.step(v.tensor_scalar(amap[:, 0:P], probs[:, 1, 0:P], coef[:, 0:1], None, ALU.mult))
                        step(v.tensor_scalar(amap[:, P:3 * P], probs[:, 1, P:3 * P], coef[:, 1:2], None, ALU.mult))
                        v.scalar_tensor_tensor(out=amap[:, 0:P], in0=probs[:, 0, 0:P], scalar=inv[:, 0:1],
                                               in1=amap[:, 0:P], op0=ALU.mult, op1=ALU.add)
                        v.scalar_tensor_tensor(out=amap[:, P:3 * P], in0=probs[:, 0, P:3 * P], scalar=inv[:, 2:3],
                                               in1=amap[:, P:3 * P], op0=ALU.mult, op1=ALU.add).then_inc(a_ok, 1)
                        split(b * 16 + 64, i)
                    if point == 5:
                        dve.wait_ge(ssq_ok, n)
                        v.tensor_scalar(var_o, ssq_o, 1.0 / P, EPS, ALU.mult, ALU.add).then_inc(var_ok, 1)
                        dve.wait_ge(std_ok, n)
                        step(v.reciprocal(inv_o, std_o))
                        for tt in range(TT):
                            last = v.tensor_scalar(o_n[:, tt, :], bank[:, 4, tt * P:(tt + 1) * P], inv_o[:, tt:tt + 1],
                                                   None, ALU.mult)
                        last.then_inc(on_ok, 1)
                    if i == KT + AHEAD - 2:
                        dve.wait_ge(m_used, b * 16 + 80)
                        dve.wait_ge(bg_ld, b * 16 + 16)
                        for c in range(2):
                            for tt in range(TT):
                                last = v.tensor_tensor(gates[:, tt, bass.ds(b * BLK + c * BANK, BANK)], bank[:, 2 * c + tt, :],
                                                       b_gate[:, c * BANK:(c + 1) * BANK], ALU.add)
                                last.then_inc(low_free, 1)
                        dve.wait_ge(low_free, b * 4 + 8)
                        dve.sem_inc(bg_used, 1)
            chain.leave(4)

            for i in range(2):
                dve.wait_ge(mix_hi_ok, i + 1)
                v.tensor_tensor(mixT_lo[:, 4 * i:4 * i + 4, :], mixedT[:, 4 * i:4 * i + 4, :],
                                mixT_hi[:, 4 * i:4 * i + 4, :].bitcast(F32), ALU.subtract).then_inc(mix_lo_ok, 1)

            def merge(b):
                dve.wait_ge(m_used, 8 * KT + 8 * (b + 1))
                col0 = (b % 2) * BLK
                for c in range(2):
                    for tt in range(TT):
                        col = col0 + c * BANK
                        src = bank[:, 4 * (b % 2) + 2 * c + tt, :]
                        if b < 2:
                            v.tensor_tensor(merged[:, tt, col:col + BANK], src, gates[:, tt, col:col + BANK],
                                            ALU.mult).then_inc(up_free, 1)
                        else:
                            gate = gates[:, tt, D + col:D + col + BANK]
                            v.tensor_tensor(gate, src, gate, ALU.mult).then_inc(up_free, 1)
                if b >= 2:
                    dve.wait_ge(up_free, 4 * (b + 1))
                    for tt in range(TT):
                        dst = merged[:, tt, col0:col0 + BLK]
                        last = v.tensor_tensor(dst, dst, gates[:, tt, D + col0:D + col0 + BLK], ALU.add)
                    last.then_inc(merged_ok, 1)

            def low_transposed(f0):
                for g in range(f0, f0 + 4):
                    dve.wait_ge(mT_hi_ok, g + 1)
                    tiles = slice(2 * g, 2 * g + 2)
                    v.tensor_tensor(mergT_lo[:, tiles, :].rearrange("p k n -> p (k n)"), bank[:, g, :],
                                    mergT_hi[:, tiles, :].rearrange("p k n -> p (k n)").bitcast(F32),
                                    ALU.subtract).then_inc(mT_lo_ok, 1)

            def residual(b):
                dve.wait_ge(m_used, 8 * KT + 32 + KT * (b + 1))
                for tt in range(TT):
                    for c in range(2):
                        col = b * BLK + c * BANK
                        v.tensor_tensor(h[:, tt, col:col + BANK], bank[:, 4 * b + 2 * c + tt, :],
                                        x_again[:, tt, col:col + BANK], ALU.add).then_inc(h_ok, 1)
                for tt in range(TT):
                    dve.wait_ge(h_ok, 4 * b + 2 * tt + 2)
                    cols = slice(b * BLK, (b + 1) * BLK)
                    v.tensor_tensor(hg[:, tt, cols], h[:, tt, cols], gain_ffn[:, cols], ALU.mult).then_inc(hg_ok, 1)

            for i in range(AHEAD, 64):
                split(8 * KT, i)
                if i == 9:
                    dve.wait_ge(oT_hi_ok, 1)
                    v.tensor_tensor(oT_lo[:], oT[:], oT_hi[:].bitcast(F32), ALU.subtract).then_inc(oT_lo_ok, 1)
                    dve.wait_ge(sig_ok, 4)
                    dve.wait_ge(bank7_free, HEADS + 1)
                if i < 36 and i % 8 == AHEAD - 1 and i > AHEAD:
                    merge(i // 8 - 1)
                if i == 28 + AHEAD - 1:
                    low_transposed(0)
                if i == 36 + AHEAD - 1:
                    low_transposed(4)
                    dve.wait_ge(x2_ld, 16)
                    dve.wait_ge(gffn_ld, 16)
                if i == 48 + AHEAD - 1:
                    residual(0)
            residual(1)
            dve.wait_ge(ssq2, 4)
            step(v.tensor_tensor(stat[:, 8:10], ssq_h[:, 0:2], ssq_h[:, 2:4], ALU.add))
            inverse_rms(ssq2, 8, var2, std2, inv2, D, 4)
            dve.wait_ge(inv2, 1)

            dve.wait_ge(logit_ps, 1)
            for tt in range(TT):
                chain.step(v.scalar_tensor_tensor(out=rt[:, tt, 0, 0:36], in0=bank[:, 2 + tt, 0:36],
                                                  scalar=stat[:, 14 + tt:15 + tt], in1=b_rout, op0=ALU.mult, op1=ALU.add))
            chain.settle()

            def wide(x, n):
                return x.rearrange("p (t a) -> p t a", a=1).to_broadcast([P, TT, n])

            def first_of(vals, top, n, tmp, idx, hot):
                step(v.tensor_reduce(top, vals, AX, ALU.max))
                step(v.tensor_tensor(tmp, vals, wide(top, n), ALU.is_equal))
                cols = iota[:, 0:n].rearrange("p (a n) -> p a n", a=1).to_broadcast([P, TT, n])
                step(v.scalar_tensor_tensor(out=tmp, in0=tmp, scalar=-BIG, in1=cols, op0=ALU.mult, op1=ALU.add))
                step(v.tensor_reduce(idx, tmp, AX, ALU.min))
                step(v.tensor_tensor(hot, tmp, wide(idx, n), ALU.is_equal))

            gtop, gidx = stat[:, 0:2], stat[:, 2:4]
            top1, idx1, top2, idx2 = top12[:, :, 0], idx12[:, :, 0], top12[:, :, 1], idx12[:, :, 1]
            ghot = rt[:, :, 2, 0:4]
            first_of(rt[:, :, 0, 0:4], gtop, 4, rt[:, :, 1, 0:4], gidx, ghot)
            v.tensor_tensor(rt[:, :, 1, 0:4], rt[:, :, 0, 0:4], wide(gtop, 4), ALU.subtract).then_inc(gdiff, 1)
            step(v.tensor_scalar(ghot, ghot, -NEG, NEG, ALU.mult, ALU.add))
            elog = rt[:, :, 3, 0:32]
            for tt in range(TT):
                ins = v.tensor_tensor(rt[:, tt, 3, 0:32].rearrange("p (g e) -> p g e", g=N_GROUPS),
                                      rt[:, tt, 0, 4:36].rearrange("p (g e) -> p g e", g=N_GROUPS),
                                      rt[:, tt, 2, 0:4].rearrange("p (g a) -> p g a", a=1).to_broadcast([P, N_GROUPS, 8]),
                                      ALU.add)
                chain.step(ins)
            chain.settle()
            hot1, hot2, both, tmp = rt[:, :, 4, 0:32], rt[:, :, 5, 0:32], rt[:, :, 6, 0:32], rt[:, :, 7, 0:32]
            first_of(elog, top1, 32, tmp, idx1, hot1)
            step(v.scalar_tensor_tensor(out=elog, in0=hot1, scalar=3 * NEG, in1=elog, op0=ALU.mult, op1=ALU.add))
            first_of(elog, top2, 32, tmp, idx2, hot2)
            v.tensor_tensor(both, hot1, hot2, ALU.add).then_inc(mask_ok, 1)
            v.tensor_tensor(stat[:, 18:20], top2, top1, ALU.subtract).then_inc(mdiff, 1)
            step(v.tensor_scalar(code[:], idx12, BIG, float(CAP), ALU.add, ALU.mult))
            dve.wait_ge(rank_ps, 1)
            for tt in range(TT):
                rank_row = bank[:, 5, 32 * tt:32 * tt + 32].rearrange("p (a e) -> p a e", a=1).to_broadcast([P, 2, 32])
                chain.step(v.tensor_tensor(rt[:, tt, 4:6, 0:32], rank_row, rt[:, tt, 4:6, 0:32], ALU.mult))
            chain.settle()
            step(v.tensor_reduce(rank12, rt[:, :, 4:6, 0:32], AX, ALU.add))
            step(v.tensor_tensor(code[:], code[:], rank12, ALU.add))
            step(v.tensor_scalar(over12, rank12, float(CAP), None, ALU.is_ge))
            for p in range(2, PASSES):
                step(v.scalar_tensor_tensor(out=over12, in0=rank12, scalar=float(p * CAP), in1=over12,
                                            op0=ALU.is_ge, op1=ALU.add))
            step(v.scalar_tensor_tensor(out=code[:], in0=over12, scalar=float(PAIRS * P - CAP), in1=code[:],
                                        op0=ALU.mult, op1=ALU.add))

            def one_hot():
                for tt in range(TT):
                    for j in range(2):
                        last = v.tensor_scalar(sel12[:, tt, j, :], iota[:], code[:, tt, j:j + 1], None, ALU.is_equal)
                step(last)
                v.tensor_tensor(sel[:], sel12[:, :, 0, :], sel12[:, :, 1, :], ALU.add).then_inc(sel_ok, 1)

            one_hot()
            for half in range(2):
                tiles = slice(half * KT // 2, (half + 1) * KT // 2)
                for tt in range(TT):
                    dve.wait_ge(hi_ok, tt + 1)
                    v.scalar_tensor_tensor(out=hn_lo[:, tt, tiles, :],
                                           in0=hg[:, tt, :].rearrange("p (q k) -> p k q", k=KT)[:, tiles, :],
                                           scalar=stat[:, 14 + tt:15 + tt], in1=hn_hi[:, tt, tiles, :].bitcast(F32),
                                           op0=ALU.mult, op1=ALU.subtract).then_inc(lo_ok, 1)
            dve.wait_ge(rank_ps, 2)
            step(v.tensor_reduce(stat[:, 26:27], bank[:, 4, 0:32], AX, ALU.max))
            step(v.tensor_copy(count[:], stat[:, 26:27]))
            dve.wait_ge(gexp, 1)
            step(v.tensor_reduce(stat[:, 22:24], rt[:, :, 1, 0:4], AX, ALU.add))
            step(v.reciprocal(stat[:, 22:24], stat[:, 22:24]))
            dve.wait_ge(mexp, 1)
            step(v.tensor_scalar(stat[:, 24:26], stat[:, 20:22], 1.0, None, ALU.add))
            step(v.reciprocal(stat[:, 24:26], stat[:, 24:26]))
            step(v.tensor_tensor(topw[:, :, 0], stat[:, 24:26], stat[:, 22:24], ALU.mult))
            step(v.tensor_tensor(topw[:, :, 1], topw[:, :, 0], stat[:, 20:22], ALU.mult))

            def gather_out(f_i, n, b=7):
                dve.wait_ge(gath_ps, n)
                src = bank[:, b, :].rearrange("p (a c s) -> p a c s", a=2, s=CAP)
                v.tensor_copy(xg[:, 4 * f_i:4 * f_i + 4, :, :].rearrange("p c a s -> p a c s"), src).then_inc(gath_d, 1)

            for n, f_i in enumerate(DVE_FILLS):
                gather_out(f_i, len(ACT_FILLS) + n + 1, f_i)
            dve.wait_ge(gath_d, 2)
            dve.sem_inc(route_ok, 1)
            dve.sem_inc(ysb_free, 1)

            STEPS = 6

            def pair(s, q):
                chain.enter(q, STEPS)

                def after(u):
                    kind, e, half = units[u]
                    n = s * 2 + (e + 1)
                    if kind == "gate" and half == 1:
                        dve.wait_ge(g_part, n)
                        v.tensor_tensor(g_sb[:], bank[0:CAP, 0, :], part[:], ALU.add).then_inc(g_sum, 1)
                    if kind == "up" and half == 1:
                        dve.wait_ge(u_part, n)
                        step(v.tensor_tensor(u_sb[:], bank[0:CAP, 1, :], part[:], ALU.add))
                        v.tensor_tensor(hid[:], silu_g[:], u_sb[:], ALU.mult).then_inc(hid_ok, 1)
                    if u == 2:
                        dve.wait_ge(ysb_free, s + 1)
                        dve.wait_ge(slot_ps, s + 1)
                        step(v.tensor_scalar(slot_f[:], bank[:, 6, 0:1], 4096.0, None, ALU.add))
                        step(v.tensor_copy(slot_row[:], slot_f[:]))
                    if u in (4, 8):
                        dve.wait_ge(hidT_hi, s * 2 + (u // 4))
                        e_t = u // 4 - 1
                        v.tensor_tensor(hidT[:, e_t, :, CAP:P], bank[:, 6, 0:4 * CAP].rearrange("p (k s) -> p k s", s=CAP),
                                        hidT[:, e_t, :, 0:CAP].bitcast(F32), ALU.subtract).then_inc(hidT_lo, 1)
                    if u == 5:
                        step(v.tensor_scalar(code[:], code[:], -float(P), None, ALU.add))
                        one_hot()
                    if kind == "down":
                        dve.wait_ge(y_part_ok, s * 4 + (u - 7))
                        v.tensor_tensor(y_sb[e * CAP:(e + 1) * CAP, half * BLK:(half + 1) * BLK],
                                        bank[0:CAP, 2 + 2 * half:4 + 2 * half, :].rearrange("p b n -> p (b n)"),
                                        y_part[:], ALU.add).then_inc(y_free, 1)

                for u in range(PAIR_UNITS):
                    for g in range(NG):
                        b = (u * NG + g) % NQ
                        dve.wait_ge(w_hi_ok, s * (PAIR_UNITS * NG) + (u * NG + g + 1))
                        v.tensor_tensor(w_lo[:, b, :], ring[:, u % RING, g * 1024:(g + 1) * 1024],
                                        w_hi[:, b, :].bitcast(F32), ALU.subtract).then_inc(w_lo_ok, 1)
                        if u == 1 and g == 0:
                            for f_i in range(FILLS // 2 + 1, FILLS, 2):
                                gather_out(f_i, s * FILLS + (f_i + 1), 6)
                    if u:
                        after(u - 1)
                    if u in (9, 11):
                        gather_out(u - 8, s * FILLS + (FILLS + (u - 8) + 1))
                after(PAIR_UNITS - 1)

            with dve.Fori(0, PAIRS) as s:
                pair(s, s)
            chain.leave(PAIRS)
            dve.wait_ge(route_ok, 1)
            most = dve.value_load(count[0:1, 0:1], min_val=0, max_val=TOK)
            with dve.If(most > CAP):
                with dve.Fori(0, PASSES - 1) as r:
                    chain.enter(r, PAIRS * STEPS)
                    with dve.Fori(0, PAIRS) as q:
                        pair(r * PAIRS + q + PAIRS, q)
                    chain.leave(PAIRS)

            def add_row(tt, j):
                dve.wait_ge(fetch[tt][j], 16)
                if j:
                    dve.wait_ge(fin_c, tt + 1)
                ins = v.scalar_tensor_tensor(out=h[:, tt, :], in0=fetched[:, tt, j, :], scalar=topw[:, tt, j:j + 1],
                                             in1=h[:, tt, :], op0=ALU.mult, op1=ALU.add)
                ins.then_inc(res_ok if j else fin_c, 1)

            def norm_var(tt):
                dve.wait_ge(ssq3, tt + 1)
                v.tensor_scalar(stat[:, 26 + tt:27 + tt], stat[:, 24 + tt:25 + tt], 1.0 / D, EPS,
                                ALU.mult, ALU.add).then_inc(var3, 1)

            def norm_out(tt):
                dve.wait_ge(std3, tt + 1)
                v.reciprocal(stat[:, 30 + tt:31 + tt], stat[:, 28 + tt:29 + tt]).then_inc(inv3, 1)
                dve.wait_ge(inv3, tt + 1)
                for half in range(2):
                    cols = slice(half * BLK, (half + 1) * BLK)
                    v.scalar_tensor_tensor(out=h[:, tt, cols], in0=h[:, tt, cols], scalar=stat[:, 30 + tt:31 + tt],
                                           in1=gain_out[:, cols], op0=ALU.mult, op1=ALU.mult).then_inc(fin_ok, 1)

            for tt in range(TT):
                for j in range(2):
                    add_row(tt, j)
                    if tt and not j:
                        norm_var(tt - 1)
            dve.wait_ge(gout_ld, 16)
            norm_out(0)
            norm_var(1)
            norm_out(1)


def constants():
    import math

    import numpy as np

    eye = np.eye(P, dtype=np.float32)
    pool = np.zeros((TOK, len(WINDOWS), TOK), np.float32)
    for g, w in enumerate(WINDOWS):
        for q in range(TOK):
            lo = max(0, q + 1 - w)
            pool[lo:q + 1, g, q] = np.float32(1.0) / np.float32(min(q + 1, w))
            pool[q, g, q] -= np.float32(1.0)
    n = np.arange(TOK)
    nf = np.maximum(n, 1).astype(np.float32)
    large = 16 + (np.log(nf / np.float32(16)) / np.float32(math.log(8.0)) * np.float32(16)).astype(np.int32)
    bucket = np.where(n < 16, n, np.minimum(large, 31))
    onehot = np.zeros((33, 2 * TOK), np.float32)
    for j in range(2 * TOK):
        onehot[bucket[TOK - 1 - j] if j < TOK else 32, j] = 1.0
    return {
        "c_eye": eye, "c_flip": np.ascontiguousarray(eye[::-1]), "c_pool": pool, "c_onehot": onehot,
        "c_tri": np.triu(np.ones((P, P), np.float32), 1), "c_ones": np.ones((P, P), np.float32),
        "c_rows": np.stack([np.stack([2 * (tt * P + np.arange(P)) + j - 4096 for j in range(2)], 1)
                            for tt in range(TT)], 1).astype(np.float32),
        "c_iota": np.tile(np.arange(P, dtype=np.float32), (P, 1)),
    }


def kernel(**inputs):
    import numpy as np

    import concourse.bacc as bacc
    from concourse.bass_utils import run_bass_kernel_spmd as run

    a = {k: np.asarray(x) for k, x in inputs.items()}
    laid = {
        "x": a["x"][0],
        "table": a["rel_bias_table"],
        "gain_mix": a["norm_mix_gain"][0].reshape(KT, P).T,
        "w_in": a["w_in"][0],
        "w_gate": a["w_merge_gate"][0],
        "b_gate": a["b_merge_gate"][0],
        "pool_mix": a["pool_mix"][0],
        "pool_scale": a["pool_scale"][0].reshape(8, P).T,
        "w_up_pool": a["w_up_pool"][0],
        "lam": np.stack([a["lambda_q1"][0], a["lambda_k1"][0], a["lambda_q2"][0], a["lambda_k2"][0]]),
        "subln": a["subln_gain"][0].reshape(P, 1),
        "w_up_attn": a["w_up_attn"][0],
        "w_out": a["w_out"][0],
        "gain_ffn": a["norm_ffn_gain"][0],
        "gain_fT": a["norm_ffn_gain"][0].reshape(KT, P).T,
        "w_rout": np.concatenate([a["w_router_group"][0],
                                  a["w_router_expert"][0].transpose(1, 0, 2).reshape(D, N_EXP)], axis=1),
        "b_rout": np.concatenate([a["b_router_group"][0], a["b_router_expert"][0].reshape(N_EXP)]),
        "w_e_gate": a["w_expert_gate"][0],
        "w_e_up": a["w_expert_up"][0],
        "w_e_down": a["w_expert_down"][0],
        "gain_out": a["final_norm_gain"],
    }
    laid.update(constants())
    nc = bacc.Bacc("TRN2", target_bir_lowering=False, num_devices=1)
    arrays, t = {}, {}
    for name, x in laid.items():
        x = np.ascontiguousarray(x)
        arrays["in_" + name] = x
        t[name] = nc.dram_tensor("in_" + name, x.shape, mybir.dt.from_np(x.dtype), kind="ExternalInput").ap()
    t["out"] = nc.dram_tensor("out", (TOK, D), F32, kind="ExternalOutput").ap()
    t["bias_dram"] = nc.dram_tensor("bias_dram", (HEADS, BANK), F32, kind="Internal").ap()
    t["y_tok"] = nc.dram_tensor("y_tok", (2 * TOK, D), F32, kind="Internal").ap()
    build(nc, t)
    r = run(nc, [arrays], core_ids=[0])
    return r.results[0]["out"].reshape(1, TOK, D)
```
